# Optimizing a Trainium2 kernel written in Bass

```python
import jax
import jax.numpy as jnp
from jax import lax
import numpy as np

D_MODEL = 2048
BATCH = 1
SEQ = 512
DEPTH = 1

GRID_W = 64
CTX_LEN = 256
HEAD_DIM = 64
A_WIDTH = D_MODEL // 4
B_WIDTH = 3 * D_MODEL // 8
C_WIDTH = D_MODEL - A_WIDTH - B_WIDTH
MIX_WIDTH = A_WIDTH + B_WIDTH + C_WIDTH
A_GROUPS = A_WIDTH // HEAD_DIM
B_HEADS = B_WIDTH // HEAD_DIM
C_HEADS = C_WIDTH // HEAD_DIM
CHUNK = 128
DECAY_LORA = 64
ICLR_LORA = 64
GATE_LORA = 128
B_COLS = 3 * B_WIDTH + 2 * DECAY_LORA + 2 * ICLR_LORA + GATE_LORA
IN_COLS = 2 * A_WIDTH + B_COLS + 3 * C_WIDTH
WIN_ROWS = 8
WIN_COLS = 16
D_FF = 4 * D_MODEL
N_MOD = 6
ALPHA = (2 * DEPTH) ** 0.25
BETA = (8 * DEPTH) ** -0.25
ATTN_SCALE = HEAD_DIM ** -0.5
LN_EPS = 1e-5
GN_EPS = 64e-5
NEG_INF = -1e30

kernel_name = "hybrid_gmlp_rwkv7_natten_dit_block"

def layer_norm(x, gain=None, bias=None, eps=LN_EPS):
    xf = x.astype(jnp.float32)
    mu = jnp.mean(xf, axis=-1, keepdims=True)
    var = jnp.mean(jnp.square(xf - mu), axis=-1, keepdims=True)
    y = ((xf - mu) * lax.rsqrt(var + eps)).astype(x.dtype)
    if gain is not None:
        y = y * gain + bias
    return y

def modulation(cvec, w_ada, b_ada):
    m = jnp.matmul(jax.nn.silu(cvec), w_ada) + b_ada
    return jnp.split(m[..., None, :], N_MOD, axis=-1)

def centred_conv3(z, taps):
    zp = jnp.pad(z, ((0, 0), (1, 1), (0, 0)))
    return zp[:, :-2] * taps[0] + zp[:, 1:-1] * taps[1] + zp[:, 2:] * taps[2]

def chunk_gmlp(u, v, w_s, b_s):
    bn, n, _ = u.shape
    u = jax.nn.gelu(u)
    v = layer_norm(jax.nn.gelu(v).reshape(bn, n // CHUNK, CHUNK, A_GROUPS, HEAD_DIM))
    mixed = jnp.einsum('gij,bnjgc->bnigc', w_s, v) + b_s.T[None, None, :, :, None]
    return u * mixed.reshape(bn, n, A_WIDTH)

def rwkv_project(zb, shift, w0, w2, a0, a2, g2, k_k, k_a):
    bn, n, _ = zb.shape
    zb = centred_conv3(zb, shift)
    cuts = [B_WIDTH, 2 * B_WIDTH, 3 * B_WIDTH, 3 * B_WIDTH + 2 * DECAY_LORA,
            3 * B_WIDTH + 2 * DECAY_LORA + 2 * ICLR_LORA]
    r, k, v, wd, ad, gd = jnp.split(zb, cuts, axis=-1)
    wd = wd.reshape(bn, n, 2, DECAY_LORA)
    ad = ad.reshape(bn, n, 2, ICLR_LORA)
    w_raw = w0[:, None, None, :] + jnp.einsum('bldr,drc->dblc', jnp.tanh(wd), w2)
    w_log = -jax.nn.softplus(-w_raw.astype(jnp.float32)) - 0.5
    decay = jnp.exp(-jnp.exp(w_log))
    a = jax.nn.sigmoid(a0[:, None, None, :] + jnp.einsum('bldr,drc->dblc', ad, a2))
    heads = lambda t: t.reshape(t.shape[:-1] + (B_HEADS, HEAD_DIM))
    kk = heads(k * k_k).astype(jnp.float32)
    kk = kk * lax.rsqrt(jnp.maximum(jnp.sum(kk * kk, axis=-1, keepdims=True), 1e-12))
    k_dir = k[None] * (1.0 + (a - 1.0) * k_a)
    g = jnp.matmul(jax.nn.sigmoid(gd), g2)
    return (heads(r), heads(decay), heads(k_dir), heads(v), -kk, kk[None] * heads(a), g)

def wkv_scan(r, w, k, v, a, b, s0):
    def step(s, inp):
        r_t, w_t, k_t, v_t, a_t, b_t = inp
        sa = jnp.einsum('dbhvk,dbhk->dbhv', s, a_t)
        s = s * w_t[..., None, :] + sa[..., :, None] * b_t[..., None, :] + v_t[..., :, None] * k_t[..., None, :]
        return s, jnp.einsum('dbhvk,dbhk->dbhv', s, r_t)
    s_final, y = lax.scan(step, s0, (r, w, k, v, a, b))
    return y, s_final

def bidir_wkv(r, w, k, v, a, b, s0):
    def time_major(t):
        t = jnp.stack([t[0], jnp.flip(t[1], axis=1)])
        return jnp.moveaxis(t, 2, 0).astype(jnp.float32)
    both = lambda t: jnp.broadcast_to(t, (2,) + t.shape)
    y, s_final = wkv_scan(time_major(both(r)), time_major(w), time_major(k),
                          time_major(both(v)), time_major(both(a)), time_major(b), s0)
    y = jnp.moveaxis(y, 0, 2)
    return y[0] + jnp.flip(y[1], axis=1), s_final

def rwkv_out(y, r, k_dir, v, g, r_k, gn_g, gn_b):
    bn, n = g.shape[:2]
    mu = jnp.mean(y, axis=-1, keepdims=True)
    var = jnp.mean(jnp.square(y - mu), axis=-1, keepdims=True)
    yn = ((y - mu) * lax.rsqrt(var + GN_EPS)).astype(g.dtype).reshape(bn, n, B_WIDTH) * gn_g + gn_b
    bonus = jnp.sum(r * jnp.sum(k_dir, axis=0) * r_k, axis=-1, keepdims=True) * v
    return (yn + bonus.reshape(bn, n, B_WIDTH).astype(g.dtype)) * g

def rwkv_mixer(zb_lat, zb_ctx, shift, w0, w2, a0, a2, g2, k_k, k_a, r_k, gn_g, gn_b, ctx_out):
    pc = rwkv_project(zb_ctx, shift, w0, w2, a0, a2, g2, k_k, k_a)
    pl = rwkv_project(zb_lat, shift, w0, w2, a0, a2, g2, k_k, k_a)
    s0 = jnp.zeros((2, zb_ctx.shape[0], B_HEADS, HEAD_DIM, HEAD_DIM), jnp.float32)
    y_c, s_ctx = bidir_wkv(*pc[:6], s0)
    y_l, _ = bidir_wkv(*pl[:6], s_ctx)
    out_l = rwkv_out(y_l, pl[0], pl[2], pl[3], pl[6], r_k, gn_g, gn_b)
    out_c = rwkv_out(y_c, pc[0], pc[2], pc[3], pc[6], r_k, gn_g, gn_b) if ctx_out else None
    return out_l, out_c

def neighbourhood_attention(q, k, v, k_ctx, v_ctx, rpb):
    bn, t, h, d = q.shape
    rows = t // GRID_W
    kr = min(WIN_ROWS, rows)
    ri = np.arange(rows)
    row_idx = np.clip(ri - kr // 2, 0, rows - kr)[:, None] + np.arange(kr)[None, :]
    ci = np.arange(GRID_W)
    col_start = np.clip(ci - WIN_COLS // 2, 0, GRID_W - WIN_COLS)
    col_in = (ci[None, :] >= col_start[:, None]) & (ci[None, :] < col_start[:, None] + WIN_COLS)
    dr = row_idx - ri[:, None] + WIN_ROWS - 1
    dc = np.clip(ci[None, :] - ci[:, None] + WIN_COLS - 1, 0, 2 * WIN_COLS - 2)
    bias = rpb[:, dr[:, None, :, None], dc[None, :, None, :]].astype(jnp.float32)
    bias = jnp.where(col_in[None, None, :, None, :], bias, NEG_INF)
    qg = (q * ATTN_SCALE).reshape(bn, rows, GRID_W, h, d)
    kb = k.reshape(bn, rows, GRID_W, h, d)[:, row_idx]
    vb = v.reshape(bn, rows, GRID_W, h, d)[:, row_idx]
    s_loc = jnp.einsum('brihd,brjchd->bhrijc', qg, kb).astype(jnp.float32) + bias
    s_ctx = jnp.einsum('brihd,bnhd->bhrin', qg, k_ctx).astype(jnp.float32)
    m = jnp.maximum(jnp.max(s_loc, axis=(-2, -1)), jnp.max(s_ctx, axis=-1))
    e_loc = jnp.exp(s_loc - m[..., None, None])
    e_ctx = jnp.exp(s_ctx - m[..., None])
    denom = jnp.sum(e_loc, axis=(-2, -1)) + jnp.sum(e_ctx, axis=-1)
    o = (jnp.einsum('bhrijc,brjchd->brihd', e_loc.astype(v.dtype), vb)
         + jnp.einsum('bhrin,bnhd->brihd', e_ctx.astype(v.dtype), v_ctx))
    o = (o.astype(jnp.float32) / jnp.moveaxis(denom, 1, -1)[..., None]).astype(v.dtype)
    return o.reshape(bn, t, h * d)

def context_attention(q, k, v):
    bn, n, h, d = q.shape
    s = jnp.einsum('bnhd,bmhd->bhnm', q * ATTN_SCALE, k).astype(jnp.float32)
    p = jax.nn.softmax(s, axis=-1).astype(v.dtype)
    return jnp.einsum('bhnm,bmhd->bnhd', p, v).reshape(bn, n, h * d)

def na_mixer(zc_lat, zc_ctx, rpb, ctx_out):
    heads = lambda t: t.reshape(t.shape[:-1] + (C_HEADS, HEAD_DIM))
    ql, kl, vl = [heads(t) for t in jnp.split(zc_lat, 3, axis=-1)]
    qc, kc, vc = [heads(t) for t in jnp.split(zc_ctx, 3, axis=-1)]
    out_l = neighbourhood_attention(ql, kl, vl, kc, vc, rpb)
    out_c = context_attention(qc, kc, vc) if ctx_out else None
    return out_l, out_c

def sq_relu_mlp(h, w_up, w_down):
    return jnp.matmul(jnp.square(jax.nn.relu(jnp.matmul(h, w_up))), w_down)

def setup_inputs(seed: int = 0) -> dict:
    key = jax.random.key(seed)
    ks = jax.random.split(key, 32)
    f32 = jnp.float32

    def nrm(i, shape, scale):
        return jax.random.normal(ks[i], shape, f32) * scale

    L = DEPTH
    taps = jnp.array([0.25, 0.5, 0.25], f32)[None, :, None]
    return {
        "x": nrm(0, (BATCH, SEQ, D_MODEL), 1.0),
        "c": nrm(1, (BATCH, D_MODEL), 1.0),
        "ctx": nrm(2, (BATCH, CTX_LEN, D_MODEL), 1.0),
        "c_ctx": nrm(3, (D_MODEL,), 1.0),
        "ada_w": nrm(4, (L, D_MODEL, N_MOD * D_MODEL), 0.5 * D_MODEL ** -0.5),
        "ada_b": nrm(5, (L, N_MOD * D_MODEL), 0.01),
        "w_in": nrm(6, (L, D_MODEL, IN_COLS), D_MODEL ** -0.5),
        "gm_ws": nrm(7, (L, A_GROUPS, CHUNK, CHUNK), CHUNK ** -0.5),
        "gm_bs": 1.0 + nrm(8, (L, A_GROUPS, CHUNK), 0.1),
        "rw_shift": taps + nrm(9, (L, 3, B_COLS), 0.05),
        "rw_w0": jax.random.uniform(ks[10], (L, 2, B_WIDTH), f32, -4.0, 1.0),
        "rw_w2": nrm(11, (L, 2, DECAY_LORA, B_WIDTH), DECAY_LORA ** -0.5),
        "rw_a0": nrm(12, (L, 2, B_WIDTH), 0.5),
        "rw_a2": nrm(13, (L, 2, ICLR_LORA, B_WIDTH), ICLR_LORA ** -0.5),
        "rw_g2": nrm(14, (L, GATE_LORA, B_WIDTH), GATE_LORA ** -0.5),
        "rw_kk": 0.85 + nrm(15, (L, B_WIDTH), 0.1),
        "rw_ka": 1.0 + nrm(16, (L, B_WIDTH), 0.1),
        "rw_rk": nrm(17, (L, B_HEADS, HEAD_DIM), 0.1),
        "rw_gn_g": 1.0 + nrm(18, (L, B_WIDTH), 0.1),
        "rw_gn_b": nrm(19, (L, B_WIDTH), 0.02),
        "na_rpb": nrm(20, (L, C_HEADS, 2 * WIN_ROWS - 1, 2 * WIN_COLS - 1), 0.1),
        "w_out": nrm(21, (L, MIX_WIDTH, D_MODEL), BETA * MIX_WIDTH ** -0.5),
        "ln1_g": 1.0 + nrm(22, (L, D_MODEL), 0.1),
        "ln1_b": nrm(23, (L, D_MODEL), 0.02),
        "w_up": nrm(24, (L, D_MODEL, D_FF), D_MODEL ** -0.5),
        "w_down": nrm(25, (L, D_FF, D_MODEL), BETA * D_FF ** -0.5),
        "ln2_g": 1.0 + nrm(26, (L, D_MODEL), 0.1),
        "ln2_b": nrm(27, (L, D_MODEL), 0.02),
    }

def reference(x, c, ctx, c_ctx, ada_w, ada_b, w_in, gm_ws, gm_bs, rw_shift, rw_w0, rw_w2,
              rw_a0, rw_a2, rw_g2, rw_kk, rw_ka, rw_rk, rw_gn_g, rw_gn_b, na_rpb, w_out,
              ln1_g, ln1_b, w_up, w_down, ln2_g, ln2_b):
    xl, xc = x, ctx
    b0 = 2 * A_WIDTH
    c0 = b0 + B_COLS
    for l in range(DEPTH):
        ctx_out = l < DEPTH - 1
        sh1, sc1, g1, sh2, sc2, g2 = modulation(c, ada_w[l], ada_b[l])
        csh1, csc1, cg1, csh2, csc2, cg2 = modulation(c_ctx, ada_w[l], ada_b[l])
        zl = jnp.matmul(xl * (1.0 + sc1) + sh1, w_in[l])
        zc = jnp.matmul(xc * (1.0 + csc1) + csh1, w_in[l])
        ya_l = chunk_gmlp(zl[..., :A_WIDTH], zl[..., A_WIDTH:b0], gm_ws[l], gm_bs[l])
        yb_l, yb_c = rwkv_mixer(zl[..., b0:c0], zc[..., b0:c0], rw_shift[l], rw_w0[l], rw_w2[l],
                                rw_a0[l], rw_a2[l], rw_g2[l], rw_kk[l], rw_ka[l], rw_rk[l],
                                rw_gn_g[l], rw_gn_b[l], ctx_out)
        yc_l, yc_c = na_mixer(zl[..., c0:], zc[..., c0:], na_rpb[l], ctx_out)
        mix_l = jnp.matmul(jnp.concatenate([ya_l, yb_l, yc_l], axis=-1), w_out[l])
        xl = layer_norm(ALPHA * xl + g1 * mix_l, ln1_g[l], ln1_b[l])
        xl = layer_norm(ALPHA * xl + g2 * sq_relu_mlp(xl * (1.0 + sc2) + sh2, w_up[l], w_down[l]),
                        ln2_g[l], ln2_b[l])
        if ctx_out:
            ya_c = chunk_gmlp(zc[..., :A_WIDTH], zc[..., A_WIDTH:b0], gm_ws[l], gm_bs[l])
            mix_c = jnp.matmul(jnp.concatenate([ya_c, yb_c, yc_c], axis=-1), w_out[l])
            xc = layer_norm(ALPHA * xc + cg1 * mix_c, ln1_g[l], ln1_b[l])
            xc = layer_norm(ALPHA * xc + cg2 * sq_relu_mlp(xc * (1.0 + csc2) + csh2, w_up[l], w_down[l]),
                            ln2_g[l], ln2_b[l])
    return xl


_drawn_inputs = setup_inputs


def setup_inputs(seed=0):
    import zlib

    import numpy as np

    out = dict(_drawn_inputs(seed))
    spreads = {}
    factors = {'ctx': 5.146,
     'c_ctx': 2.988,
     'ada_b': 6.391,
     'gm_bs': 8.0,
     'rw_w2': 7.764,
     'rw_a0': 5.632,
     'rw_a2': 4.008,
     'rw_kk': 18.363,
     'rw_ka': 6.3,
     'rw_rk': 3.594,
     'rw_gn_g': 8.0,
     'rw_gn_b': 64.0,
     'na_rpb': 64.0,
     'ln1_b': 2.867,
     'ln2_b': 2.841}
    for name, (base, spread) in spreads.items():
        noise = np.random.default_rng([zlib.crc32(name.encode()), seed]).standard_normal(out[name].shape)
        drawn = base * np.exp(spread * noise) if base else spread * noise
        out[name] = jnp.asarray(drawn.astype(out[name].dtype))
    for name, factor in factors.items():
        out[name] = (out[name] * factor).astype(out[name].dtype)
    return out
```

```python
from contextlib import ExitStack

import numpy as np

import concourse.bass as bass
from concourse import mybir

F32 = mybir.dt.float32
U32 = mybir.dt.uint32
ALU = mybir.AluOpType
ACT = mybir.ActivationFunctionType
AX = mybir.AxisListType

P = 128
D = 2048
KT = D // P
SEQ, CTX = 512, 256
TOK = CTX + SEQ
NCH = TOK // P
CCH = CTX // P
HD = 64
APAIRS, BPAIRS, CPAIRS = 4, 6, 6
DFF = 8192
TILE = KT * P
ADA_TILES = 6 * KT
RING1, RING2 = 3, 4
N1 = ADA_TILES + 3 + 3 * BPAIRS + 3 * CPAIRS + 2 * APAIRS
QFF = 4
N2 = KT + QFF * 2 * KT
ALPHA = 2.0 ** 0.25
CDEC = float(np.exp(-0.5)) / 2
GRID_W, ROWS, QC, WC = 64, 8, 16, 32
WIN0 = [0, 8, 24, 32]
NPAR = 18
LEVELS = [2, 4, 8, 16, 32, 64]
NG = NCH * 2 // 4
ZW = TOK + 4
Z_CTX, Z_LAT = 1, CTX + 3
ARENA = 52900
SMALL_BOTH, SMALL_FIRST, SMALL_B = 2 * P, 32 + ADA_TILES + 9 + P, 512 + 14 * P + BPAIRS * NPAR
ORDER = [[0, 1, 2, 3, 4, 5], [1, 0, 5, 4, 3, 2]]
PRIME, PRIME2 = 1, 4
POS_LORA = ADA_TILES
POS_B = POS_LORA + 3
POS_C = POS_B + 3 * BPAIRS
POS_A = POS_C + 3 * CPAIRS
B_PER = dict(lw=16, zero=5, done=1, dir=2, gm0=8, ctx=2, pev=5, sq=1, ss=1, ssmax=2, norm=1, kkn=1, convk=1, convv=1,
             convr=1, tp=7, tpe=7, lps=4, tanh=4, scan=4, exps=2, hats=2, xi=4, gram=6, gramev=6, gv=6, gve=6, gvc=2,
             yk=4, tmm=36, tev=36, dmm=36, dev=36, zw=2, zwe=6, umm=10, uev=10, mmm=10, mev=10, ymm=8, rk=1, ym=1,
             bonus=1, gate=1, ysq=1, yc=1, yvar=1, ystd=1, vch=40)
C_PER = dict(mask=16, bias=16, biasm=2, ctx=2, pev=5, vwp=1, vwe=1, smm=8, sadd=8, max=8, exp=8, pn=8, tp=8, tpe=8,
             pv=8, done=1, vch=8)
A_PER = dict(w=16, pev=2, tp=1, tpe=1, var=1, std=1, ln=1, mix=1, done=1, vch=3)
E_PER = dict(x=16, ln=32, ln2row=32, gcb=32, gmm=32, grow=32, omm=12, oev=16, var=8, std=8, ln1=4, htp=16, hev=16,
             uev=16, usq=16, dmm=12, dev=16, qch=16, vch=0, fin=4, stored=64)


class Turn:

    def __init__(self, eng, j, tick, chain=None, per=0):
        self.eng, self.j, self.tick, self.chain, self.per, self.n = eng, j, tick, chain, per, 0

    def wait(self, sem, per, n):
        if isinstance(self.j, int):
            self.eng.wait_ge(sem, self.j * per + n)
        else:
            self.eng.wait_ge(sem, self.j * per + n)
            self.eng.sem_inc(self.tick, 1)

    def step(self, ins):
        self.n += 1
        ins.then_inc(self.chain, 1)
        self.wait(self.chain, self.per, self.n)


def build_block(nc, stream1, stream2, xT, ctxT, xtok, small, bias, lnrows, loraw, out):
    with ExitStack() as es:
        sem = lambda n: es.enter_context(nc.semaphore(n))
        arena = es.enter_context(nc.sbuf_tensor("arena", [P, ARENA], F32))
        banks = [es.enter_context(nc.psum_tensor(f"bank{i}", [P, 512], F32)) for i in range(8)]
        top = [0]

        def take(n):
            a = arena[:, top[0]:top[0] + n]
            top[0] += n
            assert top[0] <= ARENA, top[0]
            return a

        small_s = take(SMALL_BOTH)
        ident = small_s[:, 0:P]
        ones_head = small_s[:, P:2 * P]
        mixT = take(KT * SEQ).rearrange("p (k t) -> p k t", k=KT)
        mod = take(ADA_TILES * 2)
        modv = mod.rearrange("p (c k s) -> p c k s", c=6, s=2)
        scl1 = take(2 * KT).rearrange("p (k s) -> p k s", s=2)
        scl2 = take(KT)
        eps_ln, eps_gn = take(1), take(1)
        half_top = top[0]
        ring = [take(TILE) for _ in range(RING1)]
        ringk = [r.rearrange("p (k n) -> p k n", k=KT) for r in ring]
        xm = take(KT * SEQ).rearrange("p (k t) -> p k t", k=KT)
        cm = take(KT * CTX).rearrange("p (k t) -> p k t", k=KT)
        small2 = take(SMALL_FIRST)
        csil = take(KT * 2).rearrange("p (k s) -> p k s", k=KT)
        cth = take(KT * 2)
        cin, adab_s, lp = small2[:, 0:32], small2[:, 32:128], small2[:, 128:137]
        ones_row = small2[:, 137:265]
        tw, ta = take(TOK), take(TOK)
        sgd = take(SEQ)
        zpad = [take(ZW), take(ZW), take(SEQ + 2)]
        phase_top = top[0]
        small3 = take(SMALL_B)
        gmask = small3[:, 0:512].rearrange("p (d m n) -> p d m n", d=2, m=2)
        lmask = small3[:, 512:512 + 14 * P].rearrange("p (l d n) -> p l d n", l=7, d=2)
        parall = small3[:, 512 + 14 * P:]
        pc, pch = take(NPAR), take(6)
        lw = take(3 * P)
        cK, cV, KKN, cR, KS = take(TOK), take(TOK), take(TOK), take(SEQ), take(SEQ)
        AH, RH, BH, KH = take(TOK), take(SEQ), take(TOK), take(TOK)
        GVS, ZS, WT = AH, BH, KH
        AT, BT, KTT, VT = (take(TOK) for _ in range(4))
        LT = take(12 * P)
        RB = take(8 * P)
        GT, RK = take(4 * P), take(4 * P)
        X, XT, TT = take(12 * P), take(12 * P), take(12 * P)
        t0, t1 = TT[:, 0:TOK], TT[:, TOK:2 * TOK]
        t2, t3 = X[:, 0:TOK], X[:, TOK:2 * TOK]
        t4, t5 = XT[:, 0:TOK], XT[:, TOK:2 * TOK]
        units = lambda a: a.rearrange("p (i h n) -> p i h n", h=2, n=P)
        NK = GT[:, 0:NCH * HD]
        Y = take(SEQ)
        MB = [take(P), take(P)]
        US, MQ = RK[:, 0:P], RK[:, P:P + HD]
        smid, sdif, e1, e2, pp = (take(NCH) for _ in range(5))
        top[0] = phase_top
        cmask_s = take(4 * 256)
        bias_s = take(8 * 256).rearrange("p (t h n) -> p t h n", t=4, h=2)
        qs, ks, vs = take(SEQ), take(TOK), take(CTX + 1024)
        vw = take(10 * P).rearrange("p (c n) -> p c n", c=10)
        S = [take(512) for _ in range(2)]
        PR = [take(512) for _ in range(2)]
        PT = [take(512).rearrange("p (c q) -> p c q", c=4) for _ in range(2)]
        negmax, esum, erec = take(8), take(8), take(8)
        amix_s = take(8 * P + APAIRS * P)
        agb_s = amix_s[:, 8 * P:]
        gu, gv = take(SEQ), take(SEQ)
        vt, vn, gtmp = take(SEQ), take(SEQ), take(SEQ)
        ast, amv, ars = take(48), take(16), take(8)
        top[0] = half_top
        ring2 = [take(TILE) for _ in range(RING2)]
        xr = take(4 * D).rearrange("p (m n) -> p m n", m=4)
        hT = take(KT * SEQ).rearrange("p (k t) -> p k t", k=KT)
        hid = take(KT * SEQ).rearrange("p (k t) -> p k t", k=KT)
        grow, lng, lnb = take(D), take(D), take(D)
        etmp = [take(512) for _ in range(2)]
        st2 = take(4 * 24).rearrange("p (m s) -> p m s", m=4)
        mv2 = take(8).rearrange("p (m s) -> p m s", m=4)
        rs2 = take(4)
        gcb = [take(P), take(P)]
        dtmp = [take(512) for _ in range(2)]

        tick = sem("sequencer_ticks")
        loaded = [sem(f"ring_slot_{b}_loaded") for b in range(RING1)]
        loaded2 = [sem(f"ring2_slot_{b}_loaded") for b in range(RING2)]
        slot_used = sem("weight_tiles_used")
        slot2_used = sem("weight_tiles_used_second_half")
        setup, setx = sem("small_inputs_loaded"), sem("token_inputs_loaded")
        v_setup, a_setup = sem("vector_setup_steps"), sem("scalar_setup_steps")
        mod_ev, v_mod = sem("modulation_copied"), sem("modulation_scales_ready")
        xm_ready, cm_ready = sem("latents_modulated"), sem("context_modulated")
        lora_ctx, lora_ev, lora_v = sem("lora_context_products"), sem("lora_products_copied"), sem("lora_convolved")
        lora_ready = sem("lora_inputs_ready")
        B = {n: sem("b_" + n) for n in B_PER}
        C = {n: sem("c_" + n) for n in C_PER}
        A = {n: sem("a_" + n) for n in A_PER}
        E = {n: sem("e_" + n) for n in E_PER}
        Q = banks[2:]
        PA, PB = banks[0], banks[1]
        lat = slice(CTX, TOK)

        def tokc(i):
            return slice(P * i, P * i + P)

        block = es.enter_context(nc.Block())

        @block.sync
        def _(sp):
            sp.dma_start(small_s, small["both"]).then_inc(setup, 16)
            sp.dma_start(small2, small["first"]).then_inc(setup, 16)
            sp.dma_start(small3, small["b"]).then_inc(setup, 16)
            for b in range(RING1):
                sp.dma_start(ring[b], stream1[b]).then_inc(loaded[b], 16)
            sp.dma_start(xm, xT).then_inc(setx, 16)
            sp.dma_start(cm, ctxT).then_inc(setx, 16)
            with sp.Fori(1, N1 // RING1) as s:
                for b in range(RING1):
                    sp.wait_ge(slot_used, s * RING1 + (b - RING1 + 1))
                    sp.dma_start(ring[b][:, None, :], stream1[bass.ds(s * RING1 + b, 1)].rearrange("o p n -> p o n")
                                 ).then_inc(loaded[b], 16)
            for b in range(N1 % RING1):
                sp.wait_ge(slot_used, N1 // RING1 * RING1 + b - RING1 + 1)
                sp.dma_start(ring[b], stream1[N1 // RING1 * RING1 + b]).then_inc(loaded[b], 16)
            sp.wait_ge(A["done"], 1 + APAIRS)
            sp.wait_ge(slot_used, N1)
            for b in range(RING2):
                sp.dma_start(ring2[b], stream2[b]).then_inc(loaded2[b], 16)
            sp.dma_start(xr, xtok).then_inc(E["x"], 16)
            sp.dma_start(lng, lnrows[0:1, :].to_broadcast([P, D])).then_inc(E["ln"], 16)
            sp.dma_start(lnb, lnrows[1:2, :].to_broadcast([P, D])).then_inc(E["ln"], 16)
            with sp.Fori(1, KT // RING2) as s:
                for b in range(RING2):
                    sp.wait_ge(slot2_used, s * RING2 + (b - RING2 + 1))
                    sp.dma_start(ring2[b][:, None, :], stream2[bass.ds(s * RING2 + b, 1)].rearrange("o p n -> p o n")
                                 ).then_inc(loaded2[b], 16)
            with sp.Fori(KT // RING2, N2 // RING2) as s:
                for b in range(RING2):
                    sp.wait_ge(slot2_used, s * RING2 + (b - RING2 + 1))
                    sp.dma_start(ring2[b][:, None, :], stream2[bass.ds(s * RING2 + b, 1)].rearrange("o p n -> p o n")
                                 ).then_inc(loaded2[b], 16)
            for m in range(4):
                sp.wait_ge(E["fin"], m + 1)
                sp.dma_start(out[m], xr[:, m, :]).then_inc(E["stored"], 16)
            sp.wait_ge(E["stored"], 64)

        @block.gpsimd
        def _(pool):
            nc.gpsimd.memset(zpad[0], 0.0).then_inc(B["zero"], 1)
            nc.gpsimd.memset(zpad[1], 0.0).then_inc(B["zero"], 1)
            nc.gpsimd.memset(zpad[2], 0.0).then_inc(B["zero"], 1)
            nc.gpsimd.memset(MB[0], 0.0).then_inc(B["zero"], 1)
            nc.gpsimd.memset(MB[1], 0.0).then_inc(B["zero"], 1)
            with pool.Fori(0, BPAIRS) as j:
                t = Turn(pool, j, tick)
                t.wait(B["done"], 1, 1)
                pool.dma_start(lw[:, None, :], loraw[bass.ds(j, 1)].rearrange("o p n -> p o n")).then_inc(B["lw"], 16)
                for d in range(2):
                    t.wait(B["dir"], 2, d + 1)
                    nc.gpsimd.memset(LT, 0.0).then_inc(B["gm0"], 1)
                    nc.gpsimd.memset(RB, 0.0).then_inc(B["gm0"], 1)
                    nc.gpsimd.memset(GT, 0.0).then_inc(B["gm0"], 1)
                    nc.gpsimd.memset(RK, 0.0).then_inc(B["gm0"], 1)
            pool.wait_ge(B["done"], 1 + BPAIRS)
            pool.dma_start(cmask_s, small["cmask"]).then_inc(C["mask"], 16)
            pool.dma_start(amix_s, small["amix"]).then_inc(A["w"], 16)
            pool.wait_ge(C["mask"], 16)
            cm4 = cmask_s.rearrange("p (t n) -> p t n", t=4)
            with pool.Fori(0, CPAIRS) as j:
                t = Turn(pool, j, tick)
                t.wait(C["done"], 1, 1)
                pool.dma_start(bias_s.rearrange("p t h n -> p (t h n)")[:, None, :],
                               bias[bass.ds(j, 1)].rearrange("o p n -> p o n")).then_inc(C["bias"], 16)
                t.wait(C["bias"], 16, 16)
                for h in range(2):
                    nc.gpsimd.tensor_tensor(bias_s[:, :, h, :], bias_s[:, :, h, :], cm4, ALU.add
                                            ).then_inc(C["biasm"], 1)
            pool.wait_ge(E["ln1"], 4)
            pool.dma_start(lng, lnrows[2:3, :].to_broadcast([P, D])).then_inc(E["ln2row"], 16)
            pool.dma_start(lnb, lnrows[3:4, :].to_broadcast([P, D])).then_inc(E["ln2row"], 16)

        def project(t, sems, pos, per, q, cbank, lbank, ctx_free, lat_free):
            pe = t.eng
            w = ringk[q % RING1]
            t.wait(loaded[q % RING1], 16 * per // RING1, 16 * ((pos + q) // RING1 + 1))
            if cbank is not None:
                ctx_free()
                for k in range(KT):
                    mm = pe.matmul(cbank[:, 0:CTX], w[:, k, :], cm[:, k, :], start=k == 0, stop=k == KT - 1)
                mm.then_inc(sems, 1)
            lat_free()
            for k in range(KT):
                mm = pe.matmul(lbank[:, :], w[:, k, :], xm[:, k, :], start=k == 0, stop=k == KT - 1)
            mm.then_inc(slot_used, 1)

        def project3(t, ctxsem, evsem, pos):
            ev = lambda n: (lambda: t.wait(evsem, 5, n))
            project(t, ctxsem, pos, 3, 0, PA, PB, ev(0 + PRIME), ev(0 + PRIME))
            project(t, ctxsem, pos, 3, 1, PA, PB, ev(1 + PRIME), ev(2 + PRIME))
            project(t, ctxsem, pos, 3, 2, None, PA, None, ev(3 + PRIME))

        def pe_rwkv(t):
            pe = t.eng
            w = lambda n, k: t.wait(B[n], B_PER[n], k)
            project3(t, B["ctx"], B["pev"], POS_B)
            w("sq", 1)
            w("done", 1)
            for n in range(2):
                mm = pe.matmul(Q[n][:, 0:384], ones_head, t1[:, 384 * n:384 * n + 384], start=True, stop=True)
            mm.then_inc(B["ss"], 1)
            w("convv", 1)
            for i in range(NCH):
                mm = pe.transpose(Q[2 + i // 4][:, P * (i % 4):P * (i % 4) + P], cV[:, tokc(i)], ident)
            mm.then_inc(B["tp"], 1)
            w("lw", 16)
            for d in range(2):
                h64 = slice(64 * d, 64 * d + 64)
                if d:
                    w("dir", 2)
                else:
                    w("tpe", 1)
                    w("ssmax", 2)
                for n in range(2):
                    mm = pe.matmul(Q[n][:, 0:384], lw[h64, 0:P], tw[h64, 384 * n:384 * n + 384], start=True, stop=True)
                mm.then_inc(B["lps"], 1)
                for n in range(2):
                    mm = pe.matmul(Q[2 + n][:, 0:384], lw[h64, P:2 * P], ta[h64, 384 * n:384 * n + 384], start=True, stop=True)
                mm.then_inc(B["lps"], 1)
                w("tanh", 2 * d + 2)
                w("hats", d + 1)
                for n, src in enumerate((AH, BH, KH)):
                    for i in range(NCH):
                        mm = pe.transpose(Q[2 * n + i // 4][:, P * (i % 4):P * (i % 4) + P], src[:, tokc(i)], ident)
                    mm.then_inc(B["tp"], 1)
                w("tpe", 3 * d + 4)
                for g in range(NG):
                    if g:
                        w("gramev", 3 * d + g)
                        w("gve", 3 * d + g)
                        if g > 1:
                            w("yk", 2 * d + 1)
                    for h in range(2):
                        hs = slice(64 * h, 64 * h + 64)
                        for n in range(2):
                            tk = tokc(2 * g + n)
                            lk = slice((2 * g + n - CCH) * P, (2 * g + n - CCH + 1) * P)
                            pe.matmul(Q[h][:, P * n:P * n + P], BH[hs, tk], AH[hs, tk], start=True, stop=True)
                            pe.matmul(Q[2 + h][:, P * n:P * n + P], KH[hs, tk], AH[hs, tk], start=True, stop=True)
                            if g:
                                pe.matmul(Q[h][:, 256 + P * n:384 + P * n], BH[hs, tk], RH[hs, lk], start=True, stop=True)
                                pe.matmul(Q[2 + h][:, 256 + P * n:384 + P * n], KH[hs, tk], RH[hs, lk], start=True, stop=True)
                            mm = pe.matmul(Q[4 + h][:, P * n:P * n + P], AH[hs, tk], BH[hs, tk], start=True, stop=True)
                    mm.then_inc(B["gram"], 1)
                    w("gramev", 3 * d + g + 1)
                    for n in range(2):
                        for h in range(2):
                            vcol = VT[:, P * (2 * g + n) + 64 * h:P * (2 * g + n) + 64 * h + 64]
                            u = 2 * n + h
                            mm = pe.matmul(Q[4][:, 64 * u:64 * u + 64], GT[:, P * u:P * u + P], vcol, start=True, stop=True)
                            if g:
                                mm = pe.matmul(Q[5][64 * h:64 * h + 64, P * n:P * n + P], vcol, RK[:, P * u:P * u + P],
                                               start=True, stop=True)
                    mm.then_inc(B["gv"], 1)
                w("gve", 3 * d + 3)
                w("yk", 2 * d + 2)
                def tmul(x):
                    l, g = divmod(x, NG)
                    if x >= 2:
                        w("tev", 18 * d + x - 1)
                    if l:
                        w("dev", 18 * d + x - NG + 1)
                    for u in range(4):
                        us = slice(P * (4 * g + u), P * (4 * g + u) + P)
                        mm = pe.matmul(Q[x % 2][:, P * u:P * u + P], LT[:, us], X[:, us], start=True, stop=True)
                    mm.then_inc(B["tmm"], 1)

                def dmul(x):
                    l, g = divmod(x, NG)
                    w("tev", 18 * d + x + 1)
                    if x >= 2:
                        w("dev", 18 * d + x - 1)
                    for u in range(4):
                        us = slice(P * (4 * g + u), P * (4 * g + u) + P)
                        if l < 5:
                            pe.matmul(Q[2 + x % 2][:, P * u:P * u + P], XT[:, us], TT[:, us], start=True, stop=True)
                        mm = pe.matmul(Q[4 + x % 2][:, P * u:P * u + P], TT[:, us], XT[:, us], start=True, stop=True)
                    mm.then_inc(B["dmm"], 1)

                for x in range(6 * NG):
                    tmul(x)
                    if x:
                        dmul(x - 1)
                dmul(6 * NG - 1)
                w("dev", 18 * d + 18)
                for i in range(NCH):
                    for h in range(2):
                        u = 2 * i + h
                        us = slice(P * u, P * u + P)
                        ch = slice(P * i + 64 * h, P * i + 64 * h + 64)
                        pe.matmul(Q[i // 4][:, P * (i % 4) + 64 * h:P * (i % 4) + 64 * h + 64], XT[:, us], GVS[:, ch],
                                  start=True, stop=True)
                        pe.matmul(Q[2 + i // 4][64 * h:64 * h + 64, P * (i % 4):P * (i % 4) + P], AT[:, ch], XT[:, us],
                                  start=True, stop=True)
                        mm = pe.matmul(Q[4][64 * h:64 * h + 64, 64 * i:64 * i + 64], KTT[:, ch], VT[:, ch],
                                       start=True, stop=True)
                mm.then_inc(B["zw"], 1)
                w("zwe", 3 * d + 3)
                for n, i in enumerate(ORDER[d]):
                    tk = tokc(i)
                    if n:
                        w("mev", 5 * d + n)
                        pe.matmul(Q[0][:, 0:P], WT[:, tk], MB[n % 2], start=True, stop=True).then_inc(B["umm"], 1)
                    if i >= CCH:
                        lk = slice((i - CCH) * P, (i - CCH + 1) * P)
                        pe.matmul(Q[5][:, lk], MB[n % 2], RH[:, lk], start=True, stop=False, skip_group_check=True)
                    if n:
                        w("uev", 5 * d + n)
                    if n < NCH - 1:
                        for h in range(2):
                            u_rhs = US[:, 64 * h:64 * h + 64] if n else ZS[:, P * i + 64 * h:P * i + 64 * h + 64]
                            mm = pe.matmul(Q[1][64 * h:64 * h + 64, 0:HD], BT[:, P * i + 64 * h:P * i + 64 * h + 64], u_rhs,
                                           start=True, stop=True)
                        mm.then_inc(B["mmm"], 1)
                    if i >= CCH:
                        for h in range(2):
                            mm = pe.matmul(Q[5][64 * h:64 * h + 64, lk], US[:, 64 * h:64 * h + 64],
                                           RB[:, P * (2 * (i - CCH) + h):P * (2 * (i - CCH) + h) + P],
                                           start=False, stop=True, skip_group_check=True)
                        if n < NCH - 1:
                            mm.then_inc(B["ymm"], 1)
                mm.then_inc(B["ymm"], 1)
            w("dir", 3)
            pe.matmul(Q[0][:, :], ones_head, Y, start=True, stop=True).then_inc(B["ym"], 1)
            w("rk", 1)
            pe.matmul(Q[2][:, :], ones_head, t3[:, 0:SEQ], start=True, stop=True).then_inc(B["bonus"], 1)
            pe.matmul(Q[3][:, :], lw[:, 2 * P:3 * P], sgd, start=True, stop=True).then_inc(B["gate"], 1)
            w("ysq", 1)
            pe.matmul(Q[1][:, :], ones_head, t1[:, 0:SEQ], start=True, stop=True).then_inc(B["yvar"], 1)

        def pe_attention(t):
            pe = t.eng
            w = lambda n, k: t.wait(C[n], C_PER[n], k)
            project3(t, C["ctx"], C["pev"], POS_C)
            w("pev", 5 + PRIME)
            w("done", 1)
            for c in range(10):
                src = vs[:, CTX + P * c:CTX + P * c + P] if c < 8 else vs[:, P * (c - 8):P * (c - 8) + P]
                mm = pe.transpose(Q[c // 4][:, P * (c % 4):P * (c % 4) + P], src, ident)
            mm.then_inc(C["vwp"], 1)
            w("vwe", 1)
            kv = ks[:, lat].rearrange("p (r c) -> p r c", c=GRID_W)

            def scores(x):
                b, h = divmod(x, 2)
                hs = slice(64 * h, 64 * h + 64)
                if x >= 2:
                    w("sadd", x - 1)
                qt = qs[hs, P * b:P * b + P]
                pe.matmul(Q[x % 2][:, 0:256], qt, kv[hs, :, WIN0[b]:WIN0[b] + WC], start=True, stop=True)
                pe.matmul(Q[x % 2][:, 256:512], qt, ks[hs, 0:CTX], start=True, stop=True).then_inc(C["smm"], 1)

            def turn(x):
                w("pn", x + 1)
                if x >= 2:
                    w("tpe", x - 1)
                for c in range(4):
                    mm = pe.transpose(Q[2 + x % 2][:, P * c:P * c + P], PR[x % 2][:, P * c:P * c + P], ident)
                mm.then_inc(C["tp"], 1)

            def values(x):
                b, h = divmod(x, 2)
                w("tpe", x + 1)
                for c in range(4):
                    src = vw[:, 2 * b + c if c < 2 else 6 + c, 64 * h:64 * h + 64]
                    mm = pe.matmul(Q[4][64 * h:64 * h + 64, P * b:P * b + P], src, PT[x % 2][:, c, :],
                                   start=c == 0, stop=c == 3)
                mm.then_inc(C["pv"], 1)

            for x in range(10):
                if x < 8:
                    scores(x)
                if 1 <= x < 9:
                    turn(x - 1)
                if x >= 2:
                    values(x - 2)

        def pe_gmlp(t):
            pe = t.eng
            j = t.j
            w = lambda n, k: t.wait(A[n], A_PER[n], k)
            pos = POS_A + 2 * j
            for q, bank in ((0, PA), (1, PB)):
                slot = (pos + q) % RING1
                pe.wait_ge(loaded[slot], 16 * ((pos + q) // RING1 + 1))
                if j:
                    pe.wait_ge(A["pev"], 2 * (j - 1) + q + 1)
                else:
                    pe.wait_ge(C["done"], 1 + CPAIRS)
                for k in range(KT):
                    mm = pe.matmul(bank[:, :], ringk[slot][:, k, :], xm[:, k, :], start=k == 0, stop=k == KT - 1)
                mm.then_inc(slot_used, 1)
            pe.wait_ge(A["pev"], 2 * j + 2)
            for n in range(4):
                mm = pe.transpose(Q[0][:, P * n:P * n + P], gv[:, P * n:P * n + P], ident)
            mm.then_inc(A["tp"], 1)
            pe.wait_ge(A["w"], 16)
            pe.wait_ge(A["ln"], j + 1)
            for n in range(4):
                for h in range(2):
                    g = 2 * j + h
                    mm = pe.matmul(Q[1][64 * h:64 * h + 64, P * n:P * n + P], vn[:, P * n + 64 * h:P * n + 64 * h + 64],
                                   amix_s[:, P * g:P * g + P], start=True, stop=True)
            mm.then_inc(A["mix"], 1)

        def pe_second_half(pe):
            def gate_row(c):
                for k in range(KT):
                    pe.wait_ge(E["gcb"], KT * c + k + 1)
                    if k >= 2:
                        pe.wait_ge(E["grow"], KT * c + k - 1)
                    pe.matmul(banks[k % 2][:, 0:P], gcb[k % 2], ident, start=True, stop=True).then_inc(E["gmm"], 1)

            gate_row(0)
            pe.wait_ge(E["grow"], KT)
            pe.wait_ge(A["done"], 1 + APAIRS)
            for n in range(4):
                for c in range(4):
                    pe.wait_ge(loaded2[c], 16 * (n + 1))
                    for m in range(4):
                        if c == 0 and n > 1:
                            pe.wait_ge(E["oev"], 4 * (n - 2) + m + 1)
                        for k in range(4):
                            mm = pe.matmul(banks[4 * (n % 2) + m][:, :], mixT[:, 4 * c + k, P * m:P * m + P],
                                           ring2[c][:, 512 * k:512 * k + 512], start=c == 0 and k == 0,
                                           stop=c == 3 and k == 3)
                        if c == 3 and m < 3:
                            mm.then_inc(E["omm"], 1)
                    mm.then_inc(slot2_used, 1)
            gate_row(1)
            for k in range(KT):
                for m in range(4):
                    if k == 0:
                        pe.wait_ge(E["ln1"], m + 1)
                    if m == 0 and k >= 2:
                        pe.wait_ge(E["hev"], k - 1)
                    mm = pe.transpose(banks[6 + k % 2][:, P * m:P * m + P], xr[:, m, P * k:P * k + P], ident)
                mm.then_inc(E["htp"], 1)
            with pe.Fori(0, QFF) as q:
                t = Turn(pe, q, tick)
                w = lambda n, k: t.wait(E[n], E_PER[n], k)
                pe.wait_ge(E["hev"], KT)
                for f in range(KT):
                    t.wait(loaded2[f % 4], 16 * 8, 16 * (4 + f // 4 + 1))
                    w("uev", f + PRIME2 - 1)
                    for k in range(KT):
                        mm = pe.matmul(banks[f % 2][:, :], ring2[f % 4][:, P * k:P * k + P], hT[:, k, :],
                                       start=k == 0, stop=k == KT - 1)
                    mm.then_inc(slot2_used, 1)
                for n in range(4):
                    for c in range(4):
                        t.wait(loaded2[c], 16 * 8, 16 * (4 + 4 + n + 1))
                        for m in range(4):
                            if n == 0 and c == 0 and m == 0:
                                w("usq", KT + PRIME2)
                            if c == 0:
                                w("dev", 4 * n + m + PRIME2 + 1 - 4)
                            for k in range(4):
                                mm = pe.matmul(banks[2 + m][:, :], hid[:, 4 * c + k, P * m:P * m + P],
                                               ring2[c][:, 512 * k:512 * k + 512], start=c == 0 and k == 0,
                                               stop=c == 3 and k == 3)
                            if c == 3 and m < 3:
                                mm.then_inc(E["dmm"], 1)
                        mm.then_inc(slot2_used, 1)

        @block.tensor
        def _(pe):
            pe.wait_ge(setup, 48)
            pe.wait_ge(a_setup, 2)
            with pe.Fori(0, ADA_TILES // 6) as s:
                t = Turn(pe, s, tick)
                for b in range(6):
                    t.wait(loaded[b % 3], 32, 16 * (b // 3 + 1))
                    if b % 3 == 0:
                        t.wait(mod_ev, 2, b // 3 + 1)
                    for k in range(KT):
                        mm = pe.matmul(banks[b // 3][:, 2 * (b % 3):2 * (b % 3) + 2], ringk[b % 3][:, k, :], csil[:, k, :],
                                       start=k == 0, stop=k == KT - 1)
                    mm.then_inc(slot_used, 1)
            pe.wait_ge(xm_ready, 1)
            pe.wait_ge(cm_ready, 1)
            t = Turn(pe, 0, tick)
            nop = lambda: None
            project(t, lora_ctx, POS_LORA, 3, 0, Q[0], Q[1], nop, nop)
            project(t, lora_ctx, POS_LORA, 3, 1, Q[2], Q[3], nop, nop)
            project(t, lora_ctx, POS_LORA, 3, 2, None, Q[4], nop, nop)
            pe.wait_ge(lora_ready, 2)
            with pe.Fori(0, BPAIRS) as j:
                pe_rwkv(Turn(pe, j, tick))
            with pe.Fori(0, CPAIRS) as j:
                pe_attention(Turn(pe, j, tick))
            for j in range(APAIRS):
                pe_gmlp(Turn(pe, j, tick))
            pe_second_half(pe)

        def act_project(t, ctxsem, evsem, used, pos, dst, scale_q, free):
            free()
            for n in range(3):
                if n < 2:
                    t.wait(ctxsem, 2, n + 1)
                    nc.scalar.activation(dst[n][0], PA[:, 0:CTX], ACT.Copy).then_inc(evsem, 1)
                    t.wait(slot_used, 3, pos + n + 1)
                    for to, of in dst[n][1]:
                        a = nc.scalar.activation(to, of, ACT.Copy)
                    a.then_inc(evsem, 1)
                else:
                    t.wait(slot_used, 3, pos + n + 1)
                    nc.scalar.activation(dst[2][0], dst[2][1], ACT.Copy, scale=scale_q).then_inc(evsem, 1)

        def act_rwkv(t):
            act = t.eng
            w = lambda n, k: t.wait(B[n], B_PER[n], k)
            dst = [(zpad[n][:, Z_CTX:Z_CTX + CTX], [(zpad[n][:, Z_LAT:Z_LAT + SEQ], PB[:, :])]) for n in range(2)]
            dst += [(zpad[2][:, 1:1 + SEQ], PA[:, :])]
            act_project(t, B["ctx"], B["pev"], None, POS_B, dst, 1.0, lambda: w("done", 1))
            w("convk", 1)
            nc.scalar.activation(t1, cK, ACT.Square, scale=pc[:, 13:14]).then_inc(B["sq"], 1)
            w("tp", 1)
            nc.scalar.copy(VT[:, 0:512], Q[2][:, :])
            nc.scalar.copy(VT[:, 512:TOK], Q[3][:, 0:256]).then_inc(B["tpe"], 1)
            w("ssmax", 2)
            nc.scalar.activation(t2, t3, ACT.Sqrt).then_inc(B["norm"], 1)
            for d in range(2):
                if d == 0:
                    w("kkn", 1)
                w("lps", 2 * d + 1)
                for n in range(2):
                    a = nc.scalar.activation(t0[:, 384 * n:384 * n + 384], Q[n][:, 0:384], ACT.Tanh, scale=0.5, bias=pch[:, d:d + 1])
                a.then_inc(B["tanh"], 1)
                w("lps", 2 * d + 2)
                for n in range(2):
                    a = nc.scalar.activation(t5[:, 384 * n:384 * n + 384], Q[2 + n][:, 0:384], ACT.Tanh, scale=0.5,
                                             bias=pch[:, 2 + d:3 + d])
                a.then_inc(B["tanh"], 1)
                w("scan", 2 * d + 2)
                inc, exc = ((t2, -CDEC), (t3, -CDEC)) if d == 0 else ((t3, CDEC), (t2, CDEC))
                nc.scalar.activation(t4, exc[0], ACT.Exp, scale=exc[1])
                nc.scalar.activation(t1[:, 0:SEQ], inc[0][:, lat], ACT.Exp, scale=inc[1])
                nc.scalar.activation(t0, inc[0], ACT.Exp, scale=-inc[1])
                nc.scalar.activation(e1, smid, ACT.Exp, scale=-CDEC)
                nc.scalar.activation(e2, sdif, ACT.Exp, scale=-CDEC).then_inc(B["exps"], 1)
                for n, dstt in enumerate((AT, BT, KTT)):
                    w("tp", 3 * d + n + 2)
                    nc.scalar.copy(dstt[:, 0:512], Q[2 * n][:, :])
                    nc.scalar.copy(dstt[:, 512:TOK], Q[2 * n + 1][:, 0:256]).then_inc(B["tpe"], 1)
                idb = ident[:, None, :].to_broadcast([P, 12, P])
                nc.scalar.copy(X.rearrange("p (u n) -> p u n", n=P), idb).then_inc(B["xi"], 1)
                nc.scalar.copy(XT.rearrange("p (u n) -> p u n", n=P), idb).then_inc(B["xi"], 1)
                for g in range(NG):
                    w("gv", 3 * d + g + 1)
                    nc.scalar.copy(TT[:, 256 * g:256 * g + 256], Q[4][:, 0:256]).then_inc(B["gve"], 1)
                w("gve", 3 * d + 3)
                nc.scalar.copy(GVS, TT[:, 0:TOK]).then_inc(B["gvc"], 1)
                w("gvc", d + 1)
                for x in range(6 * NG):
                    g = x % NG
                    w("tmm", 18 * d + x + 1)
                    nc.scalar.copy(TT[:, 512 * g:512 * g + 512], Q[x % 2][:, :]).then_inc(B["tev"], 1)
                w("zw", d + 1)
                nc.scalar.copy(ZS[:, 0:512], Q[0][:, :])
                nc.scalar.copy(ZS[:, 512:TOK], Q[1][:, 0:256]).then_inc(B["zwe"], 1)
                nc.scalar.copy(WT[:, 0:512], Q[2][:, :])
                nc.scalar.copy(WT[:, 512:TOK], Q[3][:, 0:256]).then_inc(B["zwe"], 1)
            w("yc", 1)
            nc.scalar.activation(t1[:, 0:SEQ], t0[:, 0:SEQ], ACT.Square).then_inc(B["ysq"], 1)
            w("yvar", 1)
            nc.scalar.activation(t2[:, 0:SEQ], Q[1][:, :], ACT.Sqrt, scale=1.0 / HD, bias=eps_gn).then_inc(B["ystd"], 1)

        def act_attention(t):
            act = t.eng
            w = lambda n, k: t.wait(C[n], C_PER[n], k)
            rows = PB[:, :].rearrange("p (r c) -> p r c", c=GRID_W)
            windows = [(vs[:, CTX + 256 * b:CTX + 256 * b + 256].rearrange("p (r c) -> p r c", c=WC),
                        rows[:, :, WIN0[b]:WIN0[b] + WC]) for b in range(4)]
            dst = [(ks[:, 0:CTX], [(ks[:, lat], PB[:, :])]), (vs[:, 0:CTX], windows),
                   (qs.rearrange("p (b r c) -> p r b c", b=4, c=QC), PA[:, :].rearrange("p (r b c) -> p r b c", b=4, c=QC))]
            act_project(t, C["ctx"], C["pev"], None, POS_C, dst, HD ** -0.5, lambda: w("done", 1))
            w("vwp", 1)
            for c in range(3):
                a = nc.scalar.copy(vw[:, 4 * c:min(4 * c + 4, 10), :],
                                   Q[c][:, 0:P * min(4, 10 - 4 * c)].rearrange("p (c n) -> p c n", n=P))
            a.then_inc(C["vwe"], 1)

            def expo(x):
                w("max", x + 1)
                if x >= 2:
                    w("tp", x - 1)
                nc.scalar.activation(PR[x % 2], S[x % 2], ACT.Exp, bias=negmax[:, x:x + 1],
                                     accum_out=esum[:, x:x + 1]).then_inc(C["exp"], 1)

            def turned(x):
                w("tp", x + 1)
                if x >= 2:
                    w("pv", x - 1)
                nc.scalar.copy(PT[x % 2].rearrange("p c q -> p (c q)"), Q[2 + x % 2][:, :]).then_inc(C["tpe"], 1)

            for x in range(9):
                if x < 8:
                    expo(x)
                if x >= 1:
                    turned(x - 1)

        def act_gmlp(t):
            j = t.j
            act = t.eng
            for q, (dst, bank) in enumerate(((gu, PA), (gv, PB))):
                act.wait_ge(slot_used, POS_A + 2 * j + q + 1)
                act.wait_ge(A["done"], j + 1)
                nc.scalar.activation(dst, bank[:, :], ACT.Gelu_apprx_tanh).then_inc(A["pev"], 1)
            act.wait_ge(A["tp"], j + 1)
            nc.scalar.copy(vt, Q[0][:, :]).then_inc(A["tpe"], 1)
            act.wait_ge(A["var"], j + 1)
            nc.scalar.activation(ars, amv.rearrange("p (u s) -> p u s", s=2)[:, :, 1], ACT.Sqrt, bias=eps_ln).then_inc(A["std"], 1)

        def act_second_half(act):
            act.wait_ge(A["done"], 1 + APAIRS)

            def gate_row(c):
                for k in range(KT):
                    act.wait_ge(E["gmm"], KT * c + k + 1)
                    if c and k == 0:
                        act.wait_ge(E["oev"], 16)
                    nc.scalar.copy(grow[:, P * k:P * k + P], banks[k % 2][:, 0:P]).then_inc(E["grow"], 1)

            def std(c):
                for m in range(4):
                    act.wait_ge(E["var"], 4 * c + m + 1)
                    nc.scalar.activation(rs2[:, m:m + 1], mv2[:, m, 1:2], ACT.Sqrt, bias=eps_ln).then_inc(E["std"], 1)

            gate_row(0)
            gate_row(1)
            std(0)
            for k in range(KT):
                act.wait_ge(E["htp"], k + 1)
                nc.scalar.activation(hT[:, k, :], banks[6 + k % 2][:, :], ACT.Identity, scale=scl2[:, k:k + 1],
                                     bias=modv[:, 3, k, 0:1]).then_inc(E["hev"], 1)
            with act.Fori(0, QFF) as q:
                t = Turn(act, q, tick)
                for f in range(KT):
                    t.wait(slot2_used, 32, KT + f + 1)
                    t.wait(E["usq"], KT, f + PRIME2 - 1)
                    nc.scalar.activation(etmp[f % 2], banks[f % 2][:, :], ACT.Relu).then_inc(E["uev"], 1)
            std(1)

        @block.scalar
        def _(act):
            act.wait_ge(setup, 48)
            nc.scalar.activation(cth, cin, ACT.Tanh, scale=0.5).then_inc(a_setup, 1)
            act.wait_ge(v_mod, 2)
            act.wait_ge(setx, 32)
            for k in range(KT):
                a = nc.scalar.activation(cm[:, k, :], cm[:, k, :], ACT.Identity, scale=scl1[:, k, 1:2], bias=modv[:, 0, k, 1:2])
            a.then_inc(cm_ready, 1)
            act.wait_ge(B["zero"], 5)
            for n in range(3):
                if n < 2:
                    act.wait_ge(lora_ctx, n + 1)
                    nc.scalar.copy(zpad[n][:, Z_CTX:Z_CTX + CTX], Q[2 * n][:, 0:CTX])
                act.wait_ge(slot_used, POS_LORA + n + 1)
                zl = zpad[n][:, Z_LAT:Z_LAT + SEQ] if n < 2 else zpad[2][:, 1:1 + SEQ]
                nc.scalar.copy(zl, Q[2 * n + 1 if n < 2 else 4][:, :]).then_inc(lora_ev, 1)
            act.wait_ge(lora_v, 3)
            nc.scalar.activation(tw, tw, ACT.Tanh).then_inc(lora_ready, 1)
            nc.scalar.activation(sgd, sgd, ACT.Tanh, scale=0.5).then_inc(a_setup, 1)
            with act.Fori(0, BPAIRS) as j:
                act_rwkv(Turn(act, j, tick))
            act.wait_ge(B["done"], 1 + BPAIRS)
            with act.Fori(0, CPAIRS) as j:
                act_attention(Turn(act, j, tick))
            act.wait_ge(C["done"], 1 + CPAIRS)
            for j in range(APAIRS):
                act_gmlp(Turn(act, j, tick))
            act_second_half(act)

        def dve_rwkv(t, conv):
            V = nc.vector
            dve = t.eng
            w = lambda n, k: t.wait(B[n], B_PER[n], k)
            t.step(V.tensor_copy(pc[:, None, :], parall.rearrange("p (j n) -> p j n", n=NPAR)[:, bass.ds(t.j, 1), :]))
            V.tensor_scalar(pch[:, 0:4], pc[:, 9:13], 0.5, None, ALU.mult)
            V.tensor_scalar(pch[:, 4:5], pc[:, 14:15], 0.5, None, ALU.mult)
            t.step(V.tensor_scalar(pch[:, 5:6], pc[:, 14:15], -0.5, 1.0, ALU.mult, ALU.add))
            w("pev", 2 + PRIME)
            conv(t.step, zpad[0], pc[:, 0:3], cK, False, B["convk"], TT)
            w("convk", 1)
            w("pev", 4 + PRIME)
            conv(t.step, zpad[1], pc[:, 3:6], cV, False, B["convv"], X)
            w("convv", 1)
            w("pev", 5 + PRIME)
            conv(t.step, zpad[2], pc[:, 6:9], cR, True, B["convr"], XT)
            w("convr", 1)
            w("ss", 1)
            V.tensor_scalar(t3[:, 0:384], Q[0][:, 0:384], 1e-12, None, ALU.max).then_inc(B["ssmax"], 1)
            V.tensor_scalar(t3[:, 384:TOK], Q[1][:, 0:384], 1e-12, None, ALU.max).then_inc(B["ssmax"], 1)
            w("norm", 1)
            t.step(V.reciprocal(t4, t2))
            V.scalar_tensor_tensor(KKN, cK, pc[:, 13:14], t4, ALU.mult, ALU.mult).then_inc(B["kkn"], 1)
            w("kkn", 1)
            for d in range(2):
                w("tanh", 2 * d + 1)
                t.step(V.tensor_scalar(t0, t0, 1.0, None, ALU.add))
                for i in range(NCH):
                    a = V.tensor_tensor_scan(t1[:, tokc(i)], ones_row, t0[:, tokc(i)], 0.0, ALU.mult, ALU.add)
                t.step(a)
                t1v = t1.rearrange("p (i n) -> p i n", n=P)
                t.step(V.tensor_copy(smid[:, :, None], t1v[:, :, 63:64]))
                V.tensor_tensor(sdif[:, :, None], t1v[:, :, 127:128], smid[:, :, None], ALU.subtract).then_inc(B["scan"], 1)
                t.step(V.tensor_tensor(t2.rearrange("p (i n) -> p i n", n=P), t1v, smid[:, :, None].to_broadcast([P, NCH, P]),
                                       ALU.subtract))
                V.tensor_tensor(t3, t2, t0, ALU.subtract).then_inc(B["scan"], 1)
                w("exps", d + 1)
                w("tanh", 2 * d + 2)
                t.step(V.tensor_scalar(t2, t5, pch[:, 4:5], pch[:, 5:6], ALU.mult, ALU.add))
                t.step(V.tensor_tensor(t2, t2, cK, ALU.mult))
                if d == 0:
                    V.tensor_copy(KS, t2[:, lat])
                else:
                    V.tensor_tensor(KS, KS, t2[:, lat], ALU.add)
                V.tensor_tensor(KH, t2, t0, ALU.mult)
                t.step(V.scalar_tensor_tensor(t3, t5, 1.0, KKN, ALU.add, ALU.mult))
                V.scalar_tensor_tensor(BH, t3, 0.5, t0, ALU.mult, ALU.mult)
                V.scalar_tensor_tensor(AH, KKN, -1.0, t4, ALU.mult, ALU.mult)
                V.tensor_tensor(RH, cR, t1[:, 0:SEQ], ALU.mult).then_inc(B["hats"], 1)
                pre, post = (e1, e2) if d == 0 else (e2, e1)
                t.step(V.tensor_copy(pp, e1))
                for n in range(NCH - 1):
                    a, b = ORDER[d][n], ORDER[d][n + 1]
                    ins = V.tensor_tensor(pp[:, a:a + 1], post[:, a:a + 1], pre[:, b:b + 1], ALU.mult)
                t.step(ins)
                w("gm0", 4 * d + 4)
                w("xi", 2 * d + 2)
                sm, im = gmask[:, d, 0, :].bitcast(U32), gmask[:, d, 1, :].bitcast(U32)
                bc = lambda m, k: m[:, None, :].to_broadcast([P, k, P])
                m1, m1T = lmask[:, 0, d, :].bitcast(U32), lmask[:, 0, 1 - d, :].bitcast(U32)
                for g in range(NG):
                    w("gram", 3 * d + g + 1)
                    if g:
                        w("gv", 3 * d + g)
                    for h in range(2):
                        two = lambda bank, c: bank[:, c:c + 256].rearrange("p (i n) -> p i n", n=P)
                        i2 = slice(2 * g, 2 * g + 2)
                        V.copy_predicated(units(LT)[:, i2, h, :], bc(sm, 2), two(Q[h], 0))
                        V.copy_predicated(units(XT)[:, i2, h, :], bc(m1T, 2), two(Q[h], 0))
                        V.copy_predicated(units(X)[:, i2, h, :], bc(m1, 2), two(Q[4 + h], 0))
                        ins = V.copy_predicated(units(GT)[:, :, h, :], bc(sm, 2), two(Q[2 + h], 0))
                        if g:
                            V.copy_predicated(units(RB)[:, 2 * g - 2:2 * g, h, :], bc(im, 2), two(Q[h], 256))
                            ins = V.copy_predicated(units(RK)[:, :, h, :], bc(im, 2), two(Q[2 + h], 256))
                    ins.then_inc(B["gramev"], 1)
                    if g:
                        w("gv", 3 * d + g + 1)
                        ys = Y[:, 256 * (g - 1):256 * g]
                        if d == 0:
                            V.tensor_copy(ys, Q[5][:, 0:256]).then_inc(B["yk"], 1)
                        else:
                            V.tensor_tensor(ys, Q[5][:, 0:256], ys, ALU.add).then_inc(B["yk"], 1)
                for x in range(6 * NG):
                    l, g = divmod(x, NG)
                    four = lambda a: a.rearrange("p (u n) -> p u n", n=P)
                    mX, mT = lmask[:, l + 1, d, :].bitcast(U32), lmask[:, l + 1, 1 - d, :].bitcast(U32)
                    w("dmm", 18 * d + x + 1)
                    if l < 5:
                        V.copy_predicated(four(X[:, 512 * g:512 * g + 512]), bc(mX, 4), four(Q[2 + x % 2][:, :]))
                    V.copy_predicated(four(XT[:, 512 * g:512 * g + 512]), bc(mT, 4), four(Q[4 + x % 2][:, :])).then_inc(B["dev"], 1)
                w("zw", d + 1)
                V.tensor_tensor(NK.rearrange("p (i n) -> p i n", n=HD), Q[4][:, 0:384].rearrange("p (i n) -> p i n", n=HD),
                                pp[:, :, None].to_broadcast([P, NCH, HD]), ALU.mult).then_inc(B["zwe"], 1)
                w("zwe", 3 * d + 3)
                for n, i in enumerate(ORDER[d]):
                    cur, nxt = MB[n % 2], MB[(n + 1) % 2]
                    if n:
                        w("umm", 5 * d + n)
                        V.tensor_tensor(US, Q[0][:, 0:P], ZS[:, tokc(i)], ALU.add).then_inc(B["uev"], 1)
                    if n < NCH - 1:
                        if n:
                            for h in range(2):
                                hs = slice(64 * h, 64 * h + 64)
                                ins = V.scalar_tensor_tensor(MQ[hs, :], cur[hs, hs], pp[hs, i:i + 1], NK[hs, HD * i:HD * i + HD],
                                                             ALU.mult, ALU.add)
                            t.step(ins)
                        w("mmm", 5 * d + n + 1)
                        for h in range(2):
                            hs = slice(64 * h, 64 * h + 64)
                            add = MQ[hs, :] if n else NK[hs, HD * i:HD * i + HD]
                            ins = V.scalar_tensor_tensor(nxt[hs, hs], Q[1][hs, 0:HD], pp[hs, i:i + 1], add, ALU.mult, ALU.add)
                        ins.then_inc(B["mev"], 1)
                w("ymm", 4 * d + 4)
                V.tensor_tensor(Y, Q[5][:, :], Y, ALU.add).then_inc(B["dir"], 1)
                w("dir", d + 2)
            V.scalar_tensor_tensor(t3[:, 0:SEQ], cR, pc[:, 15:16], KS, ALU.mult, ALU.mult).then_inc(B["rk"], 1)
            w("ym", 1)
            V.scalar_tensor_tensor(t0[:, 0:SEQ], Q[0][:, :], -1.0 / HD, Y, ALU.mult, ALU.add).then_inc(B["yc"], 1)
            w("yc", 1)
            w("bonus", 1)
            t.step(V.tensor_tensor(t4[:, 0:SEQ], Q[2][:, :], cV[:, lat], ALU.mult))
            w("ystd", 1)
            t.step(V.reciprocal(t5[:, 0:SEQ], t2[:, 0:SEQ]))
            t.step(V.tensor_tensor(t0[:, 0:SEQ], t0[:, 0:SEQ], t5[:, 0:SEQ], ALU.mult))
            t.step(V.tensor_scalar(t0[:, 0:SEQ], t0[:, 0:SEQ], pc[:, 16:17], pc[:, 17:18], ALU.mult, ALU.add))
            t.step(V.tensor_tensor(t0[:, 0:SEQ], t0[:, 0:SEQ], t4[:, 0:SEQ], ALU.add))
            w("gate", 1)
            V.tensor_tensor(mixT[:, bass.ds(t.j + APAIRS, 1), :], Q[3][:, None, :], t0[:, None, 0:SEQ], ALU.mult).then_inc(B["done"], 1)
            assert t.n == t.per, ("b", t.n)

        def dve_attention(t):
            V = nc.vector
            w = lambda n, k: t.wait(C[n], C_PER[n], k)
            w("biasm", 2)

            def addmax(x):
                b, h = divmod(x, 2)
                w("smm", x + 1)
                if x >= 2:
                    w("exp", x - 1)
                V.tensor_copy(S[x % 2][:, 256:512], Q[x % 2][:, 256:512])
                ins = V.tensor_tensor(S[x % 2][:, 0:256], Q[x % 2][:, 0:256], bias_s[:, b, h, :], ALU.add)
                ins.then_inc(C["sadd"], 1)
                w("sadd", x + 1)
                V.tensor_reduce(negmax[:, x:x + 1], S[x % 2], AX.X, ALU.max, negate=True).then_inc(C["max"], 1)

            def norm(x):
                w("exp", x + 1)
                t.step(V.reciprocal(erec[:, x:x + 1], esum[:, x:x + 1]))
                V.tensor_scalar(PR[x % 2], PR[x % 2], erec[:, x:x + 1], None, ALU.mult).then_inc(C["pn"], 1)

            for x in range(9):
                if x < 8:
                    addmax(x)
                if x >= 1:
                    norm(x - 1)
            w("pv", 8)
            for b in range(4):
                ins = V.tensor_copy(mixT[:, bass.ds(t.j + (APAIRS + BPAIRS), 1), :].rearrange("p o (r c) -> p (o r) c", c=GRID_W)
                                    [:, :, QC * b:QC * b + QC],
                                    Q[4][:, P * b:P * b + P].rearrange("p (r c) -> p r c", c=QC))
            ins.then_inc(C["done"], 1)
            assert t.n == t.per, ("c", t.n)

        def dve_gmlp(t):
            V = nc.vector
            j = t.j
            w = lambda n, k: t.wait(A[n], A_PER[n], k)
            if j == 0:
                t.eng.wait_ge(C["done"], 1 + CPAIRS)
            w("tpe", 1)
            for u in range(8):
                ins = V.bn_stats(ast[:, 6 * u:6 * u + 6], vt[:, HD * u:HD * u + HD])
            t.step(ins)
            for u in range(8):
                ins = V.bn_aggr(amv[:, 2 * u:2 * u + 2], ast[:, 6 * u:6 * u + 6])
            ins.then_inc(A["var"], 1)
            w("std", 1)
            t.step(V.reciprocal(ars, ars))
            for u in range(8):
                ins = V.tensor_scalar(vn[:, HD * u:HD * u + HD], vt[:, HD * u:HD * u + HD], amv[:, 2 * u:2 * u + 1], ars[:, u:u + 1],
                                      ALU.subtract, ALU.mult)
            ins.then_inc(A["ln"], 1)
            w("mix", 1)
            t.step(V.tensor_tensor(gtmp.rearrange("p (n i) -> p n i", n=4), Q[1][:, :].rearrange("p (n i) -> p n i", n=4),
                                   agb_s[:, None, P * j:P * j + P].to_broadcast([P, 4, P]), ALU.add))
            t.eng.wait_ge(A["pev"], 2 * j + 1)
            V.tensor_tensor(mixT[:, j, :], gtmp, gu, ALU.mult).then_inc(A["done"], 1)
            assert t.n == t.per, ("a", t.n)

        def dve_second_half(dve):
            V = nc.vector
            n_v = [0]

            def step(ins):
                n_v[0] += 1
                ins.then_inc(E["vch"], 1)
                dve.wait_ge(E["vch"], n_v[0])

            dve.wait_ge(A["done"], 1 + APAIRS)

            def gate_cols(c):
                for k in range(KT):
                    if k >= 2 or c:
                        dve.wait_ge(E["gmm"], KT * c + k - 1)
                    V.tensor_copy(gcb[k % 2], modv[:, 2 + 3 * c, k, 0:1].to_broadcast([P, P])).then_inc(E["gcb"], 1)

            gate_cols(0)
            dve.wait_ge(E["grow"], KT)
            dve.wait_ge(E["x"], 16)
            for n in range(4):
                for m in range(4):
                    if m < 3:
                        dve.wait_ge(E["omm"], 3 * n + m + 1)
                    else:
                        dve.wait_ge(slot2_used, 4 * n + 4)
                    cols = slice(512 * n, 512 * n + 512)
                    V.tensor_tensor(etmp[m % 2], banks[4 * (n % 2) + m][:, :], grow[:, cols], ALU.mult).then_inc(E["oev"], 1)
                    dve.wait_ge(E["oev"], 4 * n + m + 1)
                    step(V.scalar_tensor_tensor(xr[:, m, cols], xr[:, m, cols], ALPHA, etmp[m % 2], ALU.mult, ALU.add))
                    step(V.bn_stats(st2[:, m, 6 * n:6 * n + 6], xr[:, m, cols]))

            gate_cols(1)

            def norm(c, sems):
                for m in range(4):
                    V.bn_aggr(mv2[:, m, :], st2[:, m, :]).then_inc(E["var"], 1)
                for m in range(4):
                    dve.wait_ge(E["std"], 4 * c + m + 1)
                    step(V.reciprocal(rs2[:, m:m + 1], rs2[:, m:m + 1]))
                    step(V.tensor_scalar(xr[:, m, :], xr[:, m, :], mv2[:, m, 0:1], rs2[:, m:m + 1], ALU.subtract, ALU.mult))
                    step(V.tensor_tensor(xr[:, m, :], xr[:, m, :], lng, ALU.mult))
                    V.tensor_tensor(xr[:, m, :], xr[:, m, :], lnb, ALU.add).then_inc(sems, 1)
                dve.wait_ge(sems, 4)

            dve.wait_ge(E["ln"], 32)
            norm(0, E["ln1"])
            dve.wait_ge(E["htp"], KT)
            for m in range(4):
                ins = V.tensor_scalar(xr[:, m, :], xr[:, m, :], ALPHA, None, ALU.mult)
            step(ins)
            dve.wait_ge(E["grow"], 2 * KT)
            with dve.Fori(0, QFF) as q:
                t = Turn(dve, q, tick, E["qch"], 16)
                w = lambda n, k: t.wait(E[n], E_PER[n], k)
                for f in range(KT):
                    w("uev", f + 1 + PRIME2)
                    if f == 0:
                        t.wait(slot2_used, 32, KT)
                    V.tensor_tensor(hid[:, f, :], etmp[f % 2], etmp[f % 2], ALU.mult).then_inc(E["usq"], 1)
                w("usq", KT + PRIME2)
                for n in range(4):
                    cols = slice(512 * n, 512 * n + 512)
                    for m in range(4):
                        if m < 3:
                            w("dmm", 3 * n + m + 1)
                        else:
                            t.wait(slot2_used, 32, KT + KT + 4 * n + 4)
                        V.tensor_tensor(dtmp[m % 2], banks[2 + m][:, :], grow[:, cols], ALU.mult
                                        ).then_inc(E["dev"], 1)
                        w("dev", 4 * n + m + 1 + PRIME2)
                        t.step(V.tensor_tensor(xr[:, m, cols], xr[:, m, cols], dtmp[m % 2], ALU.add))
            for n in range(4):
                for m in range(4):
                    ins = V.bn_stats(st2[:, m, 6 * n:6 * n + 6], xr[:, m, 512 * n:512 * n + 512])
            step(ins)
            dve.wait_ge(E["ln2row"], 32)
            norm(1, E["fin"])


        @block.vector
        def _(dve):
            V = nc.vector
            n_v = [0]

            def step(ins):
                n_v[0] += 1
                ins.then_inc(v_setup, 1)
                dve.wait_ge(v_setup, n_v[0])

            step(V.memset(eps_ln, 1e-5))
            step(V.memset(eps_gn, 64e-5))
            for s, n in ((B["done"], 1), (B["dir"], 1), (C["done"], 1), (A["done"], 1), (mod_ev, 2), (B["pev"], PRIME),
                         (C["pev"], PRIME), (E["uev"], PRIME2), (E["dev"], PRIME2), (E["usq"], PRIME2)):
                dve.sem_inc(s, n)
            dve.wait_ge(setup, 48)
            dve.wait_ge(a_setup, 1)
            step(V.tensor_scalar(cth, cth, 1.0, 0.5, ALU.add, ALU.mult))
            V.tensor_tensor(csil.rearrange("p k s -> p (k s)"), cth, cin, ALU.mult).then_inc(a_setup, 1)
            with dve.Fori(0, ADA_TILES // 6) as s:
                for b in range(2):
                    dve.wait_ge(slot_used, s * 6 + 3 * (b + 1))
                    dve.sem_inc(tick, 1)
                    V.tensor_tensor(mod.rearrange("p (t s) -> p t s", s=2)[:, bass.ds(s * 6 + 3 * b, 3), :],
                                    banks[b][:, 0:6].rearrange("p (t s) -> p t s", s=2),
                                    adab_s.rearrange("p (t s) -> p t s", s=1)[:, bass.ds(s * 6 + 3 * b, 3), :].to_broadcast([P, 3, 2]),
                                    ALU.add).then_inc(mod_ev, 1)
            dve.wait_ge(mod_ev, 2 + ADA_TILES // 3)
            V.tensor_scalar_add(scl1[:, :, :], modv[:, 1, :, :], 1.0).then_inc(v_mod, 1)
            V.tensor_scalar_add(scl2, modv[:, 4, :, 0], 1.0).then_inc(v_mod, 1)
            dve.wait_ge(v_mod, 2)
            dve.wait_ge(setx, 32)
            for k in range(KT):
                a = V.tensor_scalar(xm[:, k, :], xm[:, k, :], scl1[:, k, 0:1], modv[:, 0, k, 0:1], ALU.mult, ALU.add)
            a.then_inc(xm_ready, 1)

            def conv(step, z, taps, dst, lat_only, last, tmp):
                n = SEQ if lat_only else TOK + 2
                step(V.tensor_scalar(tmp[:, 0:n], z[:, 0:n], taps[:, 0:1], None, ALU.mult))
                step(V.scalar_tensor_tensor(tmp[:, 0:n], z[:, 1:1 + n], taps[:, 1:2], tmp[:, 0:n], ALU.mult, ALU.add))
                if lat_only:
                    V.scalar_tensor_tensor(dst, z[:, 2:2 + n], taps[:, 2:3], tmp[:, 0:n], ALU.mult, ALU.add).then_inc(last, 1)
                else:
                    V.scalar_tensor_tensor(dst[:, 0:CTX], z[:, 2:2 + CTX], taps[:, 2:3], tmp[:, 0:CTX], ALU.mult, ALU.add)
                    V.scalar_tensor_tensor(dst[:, lat], z[:, 4 + CTX:4 + TOK], taps[:, 2:3], tmp[:, CTX + 2:TOK + 2],
                                           ALU.mult, ALU.add).then_inc(last, 1)

            for n, dst in enumerate((tw, ta, sgd)):
                dve.wait_ge(lora_ev, n + 1)
                conv(step, zpad[n], lp[:, 3 * n:3 * n + 3], dst, n == 2, lora_v, TT)
                dve.wait_ge(lora_v, n + 1)
            dve.wait_ge(a_setup, 3)
            V.tensor_scalar(sgd, sgd, 1.0, 0.5, ALU.add, ALU.mult).then_inc(lora_ready, 1)
            dve.wait_ge(B["zero"], 5)
            dve.wait_ge(lora_ready, 2)
            with dve.Fori(0, BPAIRS) as j:
                dve_rwkv(Turn(dve, j, tick, B["vch"], B_PER["vch"]), conv)
            with dve.Fori(0, CPAIRS) as j:
                dve_attention(Turn(dve, j, tick, C["vch"], C_PER["vch"]))
            for j in range(APAIRS):
                dve_gmlp(Turn(dve, j, tick, A["vch"], A_PER["vch"]))
            dve_second_half(dve)

def tiles(w):
    r, c = w.shape
    return w.reshape(r // P, P, c // P, P).transpose(2, 1, 0, 3).reshape(c // P, P, r)


def wide_tiles(w):
    r, c = w.shape
    return w.reshape(r // 512, 4, P, c // 512, 512).transpose(3, 0, 2, 1, 4).reshape(-1, P, 2048)


def window_masks():
    m = np.zeros((P, 4, ROWS, WC), np.float32)
    for b in range(4):
        for c in range(QC):
            col = QC * b + c
            start = min(max(col - 8, 0), GRID_W - 16)
            keys = WIN0[b] + np.arange(WC)
            m[c::QC, b, :, :] = np.where((keys >= start) & (keys < start + 16), 0.0, -1e30)
    return m.reshape(P, 4 * 256)


def triangles():
    p, f = np.arange(P)[:, None], np.arange(P)[None, :]
    g = np.stack([f > p, f >= p, f < p, f <= p], 1)
    out = [g.reshape(P, 512)]
    for m in [1] + LEVELS:
        out += [(p // m % 2 == 1) & (f // m == p // m - 1), (f // m % 2 == 1) & (p // m == f // m - 1)]
    return np.concatenate([np.asarray(a, np.float32) for a in out], 1)


def kernel(**inputs):
    import concourse.bacc as bacc
    from concourse.bass_utils import run_bass_kernel_spmd

    a = {k: np.asarray(v) for k, v in inputs.items()}
    f = np.ascontiguousarray
    w_in = a["w_in"][0]
    win = tiles(w_in)
    b0 = 2 * 512 // P
    c0 = b0 + 21
    col = lambda v, n: v.reshape(n, P)
    order = [b0 + 18, b0 + 19, b0 + 20]
    for j in range(BPAIRS):
        order += [b0 + 6 + j, b0 + 12 + j, b0 + j]
    for j in range(CPAIRS):
        order += [c0 + 6 + j, c0 + 12 + j, c0 + j]
    for j in range(APAIRS):
        order += [j, 4 + j]
    stream1 = np.concatenate([tiles(a["ada_w"][0]), win[order]])
    up, down = tiles(a["w_up"][0]), a["w_down"][0]
    parts = [wide_tiles(a["w_out"][0])]
    for q in range(QFF):
        parts += [up[KT * q:KT * q + KT], wide_tiles(down[D * q:D * q + D])]
    stream2 = np.concatenate(parts)
    shift = a["rw_shift"][0].reshape(3, 21, P)
    par = np.stack([*shift[:, 6:12], *shift[:, 12:18], *shift[:, 0:6], *a["rw_w0"][0].reshape(2, 6, P),
                    *a["rw_a0"][0].reshape(2, 6, P), col(a["rw_kk"][0], 6), col(a["rw_ka"][0], 6),
                    a["rw_rk"][0].reshape(6, P), col(a["rw_gn_g"][0], 6), col(a["rw_gn_b"][0], 6)], -1)
    lp = shift[:, 18:21].transpose(2, 1, 0).reshape(P, 9)
    loraw = np.concatenate([a["rw_w2"][0].reshape(P, 6, P), a["rw_a2"][0].reshape(P, 6, P), a["rw_g2"][0].reshape(P, 6, P)],
                           2).transpose(1, 0, 2)
    cvec = np.stack([a["c"][0].reshape(KT, P), a["c_ctx"].reshape(KT, P)], -1).transpose(1, 0, 2).reshape(P, 2 * KT)
    head = np.kron(np.eye(2), np.ones((HD, HD))).astype(np.float32)
    small_both = np.concatenate([np.eye(P, dtype=np.float32), head], 1)
    small_first = np.concatenate([cvec, a["ada_b"][0].reshape(ADA_TILES, P).T, lp, np.ones((P, P), np.float32)], 1)
    small_b = np.concatenate([triangles(), par.transpose(1, 0, 2).reshape(P, -1)], 1)
    agb = np.repeat(a["gm_bs"][0].reshape(APAIRS, 2, 1, P), HD, 2).reshape(APAIRS, P, P).transpose(1, 0, 2).reshape(P, -1)
    amix = np.concatenate([a["gm_ws"][0].transpose(2, 0, 1).reshape(P, 8 * P), agb], 1)
    r, c, kr, kc = np.ogrid[0:ROWS, 0:QC, 0:ROWS, 0:WC]
    per_block = []
    for b in range(4):
        dr = np.broadcast_to(kr - r + ROWS - 1, (ROWS, QC, ROWS, WC))
        dc = np.broadcast_to(np.clip(WIN0[b] + kc - QC * b - c + 15, 0, 30), (ROWS, QC, ROWS, WC))
        per_block.append(a["na_rpb"][0][:, dr, dc].reshape(6, 2, P, 256))
    bias = np.stack(per_block, 0).transpose(1, 3, 0, 2, 4).reshape(6, P, 8 * 256)
    lnrows = np.stack([a[n][0] for n in ("ln1_g", "ln1_b", "ln2_g", "ln2_b")])
    x = a["x"][0]
    arrays = dict(
        stream1=stream1, stream2=stream2, xT=x.T.reshape(KT, P, SEQ).transpose(1, 0, 2),
        ctxT=a["ctx"][0].T.reshape(KT, P, CTX).transpose(1, 0, 2), xtok=x.reshape(4, P, D).transpose(1, 0, 2),
        small_both=small_both, small_first=small_first, small_b=small_b, small_cmask=window_masks(), small_amix=amix,
        bias=bias, lnrows=lnrows, loraw=loraw)
    arrays = {k: f(v) for k, v in arrays.items()}

    nc = bacc.Bacc("TRN2", target_bir_lowering=False, num_devices=1)
    ap = {k: nc.dram_tensor(k, v.shape, F32, kind="ExternalInput").ap() for k, v in arrays.items()}
    out = nc.dram_tensor("out", (4, P, D), F32, kind="ExternalOutput").ap()
    small = {k[6:]: ap.pop(k) for k in list(ap) if k.startswith("small_")}
    build_block(nc, small=small, out=out, **ap)
    res = run_bass_kernel_spmd(nc, [arrays], core_ids=[0])
    return np.asarray(res.results[0]["out"]).reshape(1, SEQ, D)
```

```python
from contextlib import ExitStack

import numpy as np

import concourse.bass as bass
from concourse import mybir

F32 = mybir.dt.float32
F32R = mybir.dt.float32r
U32 = mybir.dt.uint32
ALU = mybir.AluOpType
ACT = mybir.ActivationFunctionType
AX = mybir.AxisListType

P = 128
D = 2048
KT = D // P
SEQ, CTX = 512, 256
TOK = CTX + SEQ
NCH = TOK // P
CCH = CTX // P
HD = 64
APAIRS, BPAIRS, CPAIRS = 4, 6, 6
DFF = 8192
TILE = KT * P
HALF = TILE // 2
ADA_TILES = 6 * KT
RING0, RING1, RING2 = 7, 3, 4
SPLIT2 = 2
FIRST_ADA = 35
CTX_TILES = 2 + 2 * BPAIRS + 2 * CPAIRS
PAD_ADA = FIRST_ADA + 5 * (CTX_TILES // 2)
N0 = PAD_ADA + CTX_TILES
N1 = 2 * (3 + 3 * BPAIRS + 3 * CPAIRS + 2 * APAIRS)
EFF = 8
FT = DFF // EFF // P
N2 = 2 * KT + EFF * 4 * FT
ALPHA = 2.0 ** 0.25
CDEC = float(np.exp(-0.5)) / 2
GRID_W, ROWS, QC, WC = 64, 8, 16, 32
WIN0 = [0, 8, 24, 32]
NPAR = 18
LEVELS = [2, 4, 8, 16, 32, 64]
NG = NCH * 2 // 4
ZW = TOK + 4
Z_CTX, Z_LAT = 1, CTX + 3
SMALL_BOTH, SMALL_FIRST, SMALL_B = 2 * P, 32 + PAD_ADA + 9 + P, 512 + 14 * P + BPAIRS * NPAR
ORDER = [[0, 1, 2, 3, 4, 5], [1, 0, 5, 4, 3, 2]]
PRIME2 = 4
GROUP_B, GROUP_C = 1, 1 + BPAIRS
B_PER = dict(lw=16, done=1, dir=2, gm0=2, sq=1, ss=1, ssmax=2, norm=1, kkn=1, convk=1, convv=1,
             convr=1, tp=7, tpe=7, lps=4, tanh=4, scan=4, exps=2, hats=2, xi=4, gram=6, gramev=6, gv=6, gve=6, gvc=2,
             yk=4, tmm=36, tev=36, dmm=36, dev=36, zw=2, zwe=6, umm=10, uev=10, mmm=10, mev=10, ymm=8, rk=1, ym=1,
             bonus=1, gate=1, ysq=1, yc=1, yvar=1, ystd=1, vch=40)
C_PER = dict(bias=16, cp=1, vwp=1, vwe=1, smm=8, sadd=8, max=8, exp=8, pn=8, tp=8, tpe=8, pv=8, done=1, vch=9)
A_PER = dict(gv=4, gu=4, tp=4, tpe=4, var=1, std=1, ln=4, mix=4, done=4, vch=0)
E_PER = dict(x=16, ln=32, ln2row=32, mixraw=16, mixh=16, mixl=16, gcb=32, gmm=32, grow=32, omm=6, oev=8, och=16, var=8, std=8,
             ln1=4, htp=16, hev=16, hch=16, hsplit=16, urelu=8, usq=8, uch=16, dmm=12, dev=16, qch=16, vch=0, fin=4, stored=64)


class Turn:

    def __init__(self, eng, j, tick, chain=None, per=0):
        self.eng, self.j, self.tick, self.chain, self.per, self.n = eng, j, tick, chain, per, 0

    def wait(self, sem, per, n):
        if isinstance(self.j, int):
            self.eng.wait_ge(sem, self.j * per + n)
        else:
            self.eng.wait_ge(sem, self.j * per + n)
            self.eng.sem_inc(self.tick, 1)

    def step(self, ins):
        self.n += 1
        ins.then_inc(self.chain, 1)
        self.wait(self.chain, self.per, self.n)


def build_block(nc, stream0, stream1, stream2, xT, ctxT, xtok, small, bias, lnrows, loraw, out):
    with ExitStack() as es:
        sem = lambda n: es.enter_context(nc.semaphore(n))
        banks = [es.enter_context(nc.psum_tensor(f"bank{i}", [P, 512], F32)) for i in range(8)]
        mixd = nc.dram_tensor("mixer_outputs", (KT, P, SEQ), F32, kind="Internal").ap()
        zctxd = nc.dram_tensor("context_projections", (CTX_TILES + 2, P, CTX), F32, kind="Internal").ap()
        n_alloc = [0]

        def take(n, dt=F32, scope=es):
            n_alloc[0] += 1
            return scope.enter_context(nc.sbuf_tensor(f"buf{n_alloc[0]}", [P, n], dt))[:, :]

        small_s = take(SMALL_BOTH)
        ident = small_s[:, 0:P]
        ones_head = small_s[:, P:2 * P]
        mod = take(PAD_ADA * 2)
        modv = mod[:, 0:2 * ADA_TILES].rearrange("p (c k s) -> p c k s", c=6, s=2)
        scl1 = take(2 * KT).rearrange("p (k s) -> p k s", s=2)
        scl2 = take(KT)
        eps_ln, eps_gn, zero = take(1), take(1), take(1)
        first = ExitStack()
        f1 = lambda n, dt=F32: take(n, dt, first)
        raw = [f1(HALF) for _ in range(RING1)]
        wh = [f1(HALF, F32R) for _ in range(RING1)]
        wl = [f1(HALF, F32R) for _ in range(RING1)]
        xh, xl = (f1(KT * SEQ, F32R).rearrange("p (k t) -> p k t", k=KT) for _ in range(2))
        small2 = f1(SMALL_FIRST)
        cin, adab_s, lp = small2[:, 0:32], small2[:, 32:32 + PAD_ADA], small2[:, 32 + PAD_ADA:41 + PAD_ADA]
        ones_row = small2[:, 41 + PAD_ADA:]
        phase = ExitStack()
        f0 = lambda n, dt=F32: take(n, dt, phase)
        ring0 = [f0(TILE) for _ in range(RING0)]
        ring0k = [r.rearrange("p (k n) -> p k n", k=KT) for r in ring0]
        cm = f0(KT * CTX).rearrange("p (k t) -> p k t", k=KT)
        xraw = f0(8 * SEQ).rearrange("p (k t) -> p k t", k=8)
        csil = f0(KT * 2).rearrange("p (k s) -> p k s", k=KT)
        cth = f0(KT * 2)
        zst = [f0(CTX), f0(CTX)]
        phase.close()
        zpad = [f1(ZW), f1(ZW), f1(SEQ + 2)]
        mst = f1(SEQ)
        phase = ExitStack()
        f0 = lambda n, dt=F32: take(n, dt, phase)
        tw, ta, sgd = f0(TOK), f0(TOK), f0(SEQ)
        small3 = f0(SMALL_B)
        gmask = small3[:, 0:512].rearrange("p (d m n) -> p d m n", d=2, m=2)
        lmask = small3[:, 512:512 + 14 * P].rearrange("p (l d n) -> p l d n", l=7, d=2)
        parall = small3[:, 512 + 14 * P:]
        pc, pch = f0(NPAR), f0(6)
        lw = f0(3 * P)
        cK, cV, KKN, cR, KS = f0(TOK), f0(TOK), f0(TOK), f0(SEQ), f0(SEQ)
        AH, RH, BH, KH = f0(TOK), f0(SEQ), f0(TOK), f0(TOK)
        GVS, ZS, WT = AH, BH, KH
        AT, BT, KTT, VT = (f0(TOK) for _ in range(4))
        LT = f0(12 * P)
        RB = f0(8 * P)
        GT, RK = f0(4 * P), f0(4 * P)
        units = lambda a: a.rearrange("p (i h n) -> p i h n", h=2, n=P)
        NK = GT[:, 0:NCH * HD]
        Y = f0(SEQ)
        MB = [f0(P), f0(P)]
        US, MQ = RK[:, 0:P], RK[:, P:P + HD]
        smid, sdif, e1, e2, pp = (f0(NCH) for _ in range(5))
        X, XT, TT = f0(12 * P), f0(12 * P), f0(12 * P)
        t0, t1 = TT[:, 0:TOK], TT[:, TOK:2 * TOK]
        t2, t3 = X[:, 0:TOK], X[:, TOK:2 * TOK]
        t4, t5 = XT[:, 0:TOK], XT[:, TOK:2 * TOK]
        phase.close()
        phase = ExitStack()
        f0 = lambda n, dt=F32: take(n, dt, phase)
        cmask_s = f0(4 * 256)
        bias_s = f0(8 * 256).rearrange("p (t h n) -> p t h n", t=4, h=2)
        qs, ks, vs = f0(SEQ), f0(TOK), f0(CTX + 1024)
        vw = f0(10 * P).rearrange("p (c n) -> p c n", c=10)
        S = [f0(512) for _ in range(2)]
        PR = [f0(512) for _ in range(2)]
        PT = [f0(512).rearrange("p (c q) -> p c q", c=4) for _ in range(2)]
        negmax, esum, erec = f0(8), f0(8), f0(8)
        amix_s = f0(8 * P + APAIRS * P)
        agb_s = amix_s[:, 8 * P:]
        gu, gv, vt, vn, gout = ([f0(SEQ) for _ in range(APAIRS)] for _ in range(5))
        ast, amv, ars = f0(4 * 48), f0(64), f0(32)
        phase.close()
        first.close()
        second = ExitStack()
        f2 = lambda n, dt=F32: take(n, dt, second)
        raw2 = [f2(HALF) for _ in range(RING2)]
        wh2 = [f2(HALF, F32R) for _ in range(SPLIT2)]
        wl2 = [f2(HALF, F32R) for _ in range(SPLIT2)]
        xr = f2(4 * D).rearrange("p (m n) -> p m n", m=4)
        hTh, hTl = (f2(KT * SEQ, F32R).rearrange("p (k t) -> p k t", k=KT) for _ in range(2))
        mixh, mixl = hTh, hTl
        grow, lng, lnb = f2(D), f2(D), f2(D)
        etmp = [f2(512) for _ in range(2)]
        dtmp = [f2(512) for _ in range(2)]
        st2 = f2(4 * 24).rearrange("p (m s) -> p m s", m=4)
        mv2 = f2(8).rearrange("p (m s) -> p m s", m=4)
        rs2 = f2(4)
        gcb = [f2(P), f2(P)]
        phase = ExitStack()
        mixraw = take(KT * SEQ, F32, phase).rearrange("p (k t) -> p k t", k=KT)
        phase.close()
        hidh, hidl = (f2(FT * SEQ, F32R).rearrange("p (k t) -> p k t", k=FT) for _ in range(2))
        second.close()

        tick = sem("sequencer_ticks")
        loaded0 = [sem(f"tile_slot_{b}_loaded") for b in range(RING0)]
        used0 = sem("whole_tiles_used")
        rawld = [sem(f"raw_slot_{b}_loaded") for b in range(RING1)]
        high, split, used1 = sem("pieces_high_part"), sem("pieces_split"), sem("pieces_used")
        rawld2 = [sem(f"raw2_slot_{b}_loaded") for b in range(RING2)]
        high2, split2, used2 = sem("pieces2_high_part"), sem("pieces2_split"), sem("pieces2_used")
        setup, setc, setxr = sem("small_inputs_loaded"), sem("context_loaded"), sem("latents_loaded")
        v_setup, a_setup = sem("vector_setup_steps"), sem("scalar_setup_steps")
        mod_ev, v_mod = sem("modulation_copied"), sem("modulation_scales_ready")
        xmod, xhigh, xsplit = sem("latents_modulated"), sem("latents_high_part"), sem("latents_split")
        cm_ready, zst_ev = sem("context_modulated"), sem("context_products_copied")
        zst_out = [sem("context_products_stored_0"), sem("context_products_stored_1")]
        z_ev, z_ctx = sem("projections_copied"), sem("context_projections_loaded")
        zeroed, bparams = sem("pads_cleared"), sem("rwkv_constants_loaded")
        lora_v, lora_ready = sem("lora_convolved"), sem("lora_inputs_ready")
        mst_out, mix_out = sem("mixer_tile_stored"), sem("gmlp_tiles_stored")
        amix_ld, cmask_ld = sem("gmlp_weights_loaded"), sem("window_masks_loaded")
        B = {n: sem("b_" + n) for n in B_PER}
        C = {n: sem("c_" + n) for n in C_PER}
        A = {n: sem("a_" + n) for n in A_PER}
        E = {n: sem("e_" + n) for n in E_PER}
        Q = banks[2:]
        PA, PB = banks[0], banks[1]
        lat = slice(CTX, TOK)

        def tokc(i):
            return slice(P * i, P * i + P)

        block = es.enter_context(nc.Block())

        @block.sync
        def _(sp):
            sp.dma_start(small_s, small["both"]).then_inc(setup, 16)
            sp.dma_start(small2, small["first"]).then_inc(setup, 16)
            for b in range(RING0):
                sp.dma_start(ring0[b], stream0[b]).then_inc(loaded0[b], 16)
            sp.dma_start(cm, ctxT).then_inc(setc, 16)
            with sp.Fori(1, N0 // RING0) as s:
                for b in range(RING0):
                    sp.wait_ge(used0, s * RING0 + (b - RING0 + 1))
                    sp.dma_start(ring0[b][:, None, :], stream0[bass.ds(s * RING0 + b, 1)].rearrange("o p n -> p o n")
                                 ).then_inc(loaded0[b], 16)
            for b in range(RING1):
                sp.dma_start(raw[b], stream1[b]).then_inc(rawld[b], 16)
            with sp.Fori(1, N1 // RING1) as s:
                for b in range(RING1):
                    sp.wait_ge(split, s * RING1 + (b - RING1 + 1))
                    sp.dma_start(raw[b][:, None, :], stream1[bass.ds(s * RING1 + b, 1)].rearrange("o p n -> p o n")
                                 ).then_inc(rawld[b], 16)
            for b in range(N1 % RING1):
                sp.wait_ge(split, N1 // RING1 * RING1 + b - RING1 + 1)
                sp.dma_start(raw[b], stream1[N1 // RING1 * RING1 + b]).then_inc(rawld[b], 16)
            sp.wait_ge(A["done"], APAIRS)
            sp.wait_ge(used1, N1)
            sp.wait_ge(mst_out, 16 * (1 + BPAIRS + CPAIRS))
            sp.wait_ge(mix_out, 16 * APAIRS)
            for b in range(RING2):
                sp.dma_start(raw2[b], stream2[b]).then_inc(rawld2[b], 16)
            sp.dma_start(mixraw, mixd.rearrange("k p t -> p k t")).then_inc(E["mixraw"], 16)
            sp.dma_start(xr, xtok).then_inc(E["x"], 16)
            sp.dma_start(lng, lnrows[0:1, :].to_broadcast([P, D])).then_inc(E["ln"], 16)
            sp.dma_start(lnb, lnrows[1:2, :].to_broadcast([P, D])).then_inc(E["ln"], 16)
            with sp.Fori(1, N2 // RING2) as s:
                for b in range(RING2):
                    sp.wait_ge(split2, s * RING2 + (b - RING2 + 1))
                    sp.dma_start(raw2[b][:, None, :], stream2[bass.ds(s * RING2 + b, 1)].rearrange("o p n -> p o n")
                                 ).then_inc(rawld2[b], 16)
            for m in range(4):
                sp.wait_ge(E["fin"], m + 1)
                sp.dma_start(out[m], xr[:, m, :]).then_inc(E["stored"], 16)
            sp.wait_ge(E["stored"], 64)

        @block.gpsimd
        def _(pool):
            G = nc.gpsimd
            for n in range(2):
                if n:
                    pool.wait_ge(xsplit, 1)
                pool.dma_start(xraw, xT[:, 8 * n:8 * n + 8, :]).then_inc(setxr, 16)
                pool.wait_ge(setxr, 16 * (n + 1))
                pool.wait_ge(v_mod, 2)
                for k in range(8):
                    g = G.tensor_scalar(xraw[:, k, :], xraw[:, k, :], scl1[:, 8 * n + k, 0:1], modv[:, 0, 8 * n + k, 0:1],
                                        ALU.mult, ALU.add)
                g.then_inc(xmod, 1)
                pool.wait_ge(xmod, n + 1)
                G.tensor_copy(xh[:, 8 * n:8 * n + 8, :], xraw).then_inc(xhigh, 1)
                pool.wait_ge(xhigh, n + 1)
                G.tensor_tensor(xl[:, 8 * n:8 * n + 8, :], xraw, xh[:, 8 * n:8 * n + 8, :].bitcast(F32), ALU.subtract
                                ).then_inc(xsplit, 1)

            def split_piece(wait, n, b):
                wait(rawld[b], 16, n, True)
                G.tensor_copy(wh[b], raw[b]).then_inc(high, 1)
                wait(high, RING1, n, False)
                G.tensor_tensor(wl[b], raw[b], wh[b].bitcast(F32), ALU.subtract).then_inc(split, 1)

            def fixed(s_, per, n, slot):
                pool.wait_ge(s_, 16 * (n // RING1 + 1) if slot else n + 1)

            for b in range(RING1):
                split_piece(fixed, b, b)
            with pool.Fori(1, N1 // RING1) as s:
                t = Turn(pool, s, tick)
                for b in range(RING1):
                    t.wait(used1, RING1, b + 1 - RING1)
                    split_piece(lambda s_, per, n, slot: t.wait(s_, per, 16 if slot else n + 1), b, b)
            for b in range(N1 % RING1):
                n = N1 // RING1 * RING1 + b
                pool.wait_ge(used1, n + 1 - RING1)
                split_piece(fixed, n, b)
            with pool.Fori(0, N2 // RING2) as s:
                t = Turn(pool, s, tick)
                for b in range(RING2):
                    t.wait(high2, RING2, b + 1)
                    G.tensor_tensor(wl2[b % SPLIT2], raw2[b], wh2[b % SPLIT2].bitcast(F32), ALU.subtract).then_inc(split2, 1)
            pool.wait_ge(E["ln1"], 4)
            pool.dma_start(lng, lnrows[2:3, :].to_broadcast([P, D])).then_inc(E["ln2row"], 16)
            pool.dma_start(lnb, lnrows[3:4, :].to_broadcast([P, D])).then_inc(E["ln2row"], 16)

        class Projection:

            def __init__(self, t, group, tiles_=3, first_tile=0):
                self.t, self.group, self.n, self.tiles, self.first = t, group, 0, tiles_, first_tile

            def parts(self, count):
                pe = self.t.eng
                for _ in range(count):
                    n = self.n
                    self.n += 1
                    q, h, sub = n // 8, n // 4 % 2, n % 4
                    bank, slot = (PA, PB)[(q + self.first) % 2], (2 * q + h) % RING1
                    if sub == 0:
                        self.t.wait(split, 6, 6 * self.group + 2 * q + h + 1)
                        free = 3 * self.group + q - (1 if self.first or q == 2 else q)
                        if h == 0 and free > 0:
                            self.t.wait(z_ev, 3, free)
                    for k in (8 * h + 2 * sub, 8 * h + 2 * sub + 1):
                        c = P * (k % 8)
                        pe.matmul(bank[:, :], wh[slot][:, c:c + P], xh[:, k, :], start=k == 0, stop=False)
                        pe.matmul(bank[:, :], wh[slot][:, c:c + P], xl[:, k, :], start=False, stop=False)
                        mm = pe.matmul(bank[:, :], wl[slot][:, c:c + P], xh[:, k, :], start=False, stop=k == KT - 1)
                    if sub == 3:
                        mm.then_inc(used1, 1)

            def rest(self):
                self.parts(8 * self.tiles - self.n)

        def pe_rwkv(t):
            pe = t.eng
            w = lambda n, k: t.wait(B[n], B_PER[n], k)
            nxt = Projection(t, GROUP_B + 1)
            nxt.parts(4)
            w("sq", 1)
            w("done", 1)
            for n in range(2):
                mm = pe.matmul(Q[n][:, 0:384], ones_head, t1[:, 384 * n:384 * n + 384], start=True, stop=True)
            mm.then_inc(B["ss"], 1)
            w("convv", 1)
            for i in range(NCH):
                mm = pe.transpose(Q[2 + i // 4][:, P * (i % 4):P * (i % 4) + P], cV[:, tokc(i)], ident)
            mm.then_inc(B["tp"], 1)
            w("lw", 16)
            for d in range(2):
                h64 = slice(64 * d, 64 * d + 64)
                if d:
                    w("dir", 2)
                else:
                    w("tpe", 1)
                    w("ssmax", 2)
                for n in range(2):
                    mm = pe.matmul(Q[n][:, 0:384], lw[h64, 0:P], tw[h64, 384 * n:384 * n + 384], start=True, stop=True)
                mm.then_inc(B["lps"], 1)
                for n in range(2):
                    mm = pe.matmul(Q[2 + n][:, 0:384], lw[h64, P:2 * P], ta[h64, 384 * n:384 * n + 384], start=True, stop=True)
                mm.then_inc(B["lps"], 1)
                nxt.parts(8 if d == 0 else 4)
                w("tanh", 2 * d + 2)
                w("hats", d + 1)
                for n, src in enumerate((AH, BH, KH)):
                    for i in range(NCH):
                        mm = pe.transpose(Q[2 * n + i // 4][:, P * (i % 4):P * (i % 4) + P], src[:, tokc(i)], ident)
                    mm.then_inc(B["tp"], 1)
                w("tpe", 3 * d + 4)
                for g in range(NG):
                    if g:
                        w("gramev", 3 * d + g)
                        w("gve", 3 * d + g)
                        if g > 1:
                            w("yk", 2 * d + 1)
                    for h in range(2):
                        hs = slice(64 * h, 64 * h + 64)
                        for n in range(2):
                            tk = tokc(2 * g + n)
                            lk = slice((2 * g + n - CCH) * P, (2 * g + n - CCH + 1) * P)
                            pe.matmul(Q[h][:, P * n:P * n + P], BH[hs, tk], AH[hs, tk], start=True, stop=True)
                            pe.matmul(Q[2 + h][:, P * n:P * n + P], KH[hs, tk], AH[hs, tk], start=True, stop=True)
                            if g:
                                pe.matmul(Q[h][:, 256 + P * n:384 + P * n], BH[hs, tk], RH[hs, lk], start=True, stop=True)
                                pe.matmul(Q[2 + h][:, 256 + P * n:384 + P * n], KH[hs, tk], RH[hs, lk], start=True, stop=True)
                            mm = pe.matmul(Q[4 + h][:, P * n:P * n + P], AH[hs, tk], BH[hs, tk], start=True, stop=True)
                    mm.then_inc(B["gram"], 1)
                    w("gramev", 3 * d + g + 1)
                    for n in range(2):
                        for h in range(2):
                            vcol = VT[:, P * (2 * g + n) + 64 * h:P * (2 * g + n) + 64 * h + 64]
                            u = 2 * n + h
                            mm = pe.matmul(Q[4][:, 64 * u:64 * u + 64], GT[:, P * u:P * u + P], vcol, start=True, stop=True)
                            if g:
                                mm = pe.matmul(Q[5][64 * h:64 * h + 64, P * n:P * n + P], vcol, RK[:, P * u:P * u + P],
                                               start=True, stop=True)
                    mm.then_inc(B["gv"], 1)
                w("gve", 3 * d + 3)
                w("yk", 2 * d + 2)
                def tmul(x):
                    l, g = divmod(x, NG)
                    if x >= 2:
                        w("tev", 18 * d + x - 1)
                    if l:
                        w("dev", 18 * d + x - NG + 1)
                    for u in range(4):
                        us = slice(P * (4 * g + u), P * (4 * g + u) + P)
                        mm = pe.matmul(Q[x % 2][:, P * u:P * u + P], LT[:, us], X[:, us], start=True, stop=True)
                    mm.then_inc(B["tmm"], 1)

                def dmul(x):
                    l, g = divmod(x, NG)
                    w("tev", 18 * d + x + 1)
                    if x >= 2:
                        w("dev", 18 * d + x - 1)
                    for u in range(4):
                        us = slice(P * (4 * g + u), P * (4 * g + u) + P)
                        if l < 5:
                            pe.matmul(Q[2 + x % 2][:, P * u:P * u + P], XT[:, us], TT[:, us], start=True, stop=True)
                        mm = pe.matmul(Q[4 + x % 2][:, P * u:P * u + P], TT[:, us], XT[:, us], start=True, stop=True)
                    mm.then_inc(B["dmm"], 1)

                for x in range(6 * NG):
                    tmul(x)
                    if x:
                        dmul(x - 1)
                dmul(6 * NG - 1)
                w("dev", 18 * d + 18)
                for i in range(NCH):
                    for h in range(2):
                        u = 2 * i + h
                        us = slice(P * u, P * u + P)
                        ch = slice(P * i + 64 * h, P * i + 64 * h + 64)
                        pe.matmul(Q[i // 4][:, P * (i % 4) + 64 * h:P * (i % 4) + 64 * h + 64], XT[:, us], GVS[:, ch],
                                  start=True, stop=True)
                        pe.matmul(Q[2 + i // 4][64 * h:64 * h + 64, P * (i % 4):P * (i % 4) + P], AT[:, ch], XT[:, us],
                                  start=True, stop=True)
                        mm = pe.matmul(Q[4][64 * h:64 * h + 64, 64 * i:64 * i + 64], KTT[:, ch], VT[:, ch],
                                       start=True, stop=True)
                mm.then_inc(B["zw"], 1)
                w("zwe", 3 * d + 3)
                for n, i in enumerate(ORDER[d]):
                    tk = tokc(i)
                    if n:
                        w("mev", 5 * d + n)
                        pe.matmul(Q[0][:, 0:P], WT[:, tk], MB[n % 2], start=True, stop=True).then_inc(B["umm"], 1)
                    if i >= CCH:
                        lk = slice((i - CCH) * P, (i - CCH + 1) * P)
                        pe.matmul(Q[5][:, lk], MB[n % 2], RH[:, lk], start=True, stop=False, skip_group_check=True)
                    if n:
                        nxt.parts(1 if d == 0 or n < 4 else 0)
                        w("uev", 5 * d + n)
                    if n < NCH - 1:
                        for h in range(2):
                            u_rhs = US[:, 64 * h:64 * h + 64] if n else ZS[:, P * i + 64 * h:P * i + 64 * h + 64]
                            mm = pe.matmul(Q[1][64 * h:64 * h + 64, 0:HD], BT[:, P * i + 64 * h:P * i + 64 * h + 64], u_rhs,
                                           start=True, stop=True)
                        mm.then_inc(B["mmm"], 1)
                    if i >= CCH:
                        for h in range(2):
                            mm = pe.matmul(Q[5][64 * h:64 * h + 64, lk], US[:, 64 * h:64 * h + 64],
                                           RB[:, P * (2 * (i - CCH) + h):P * (2 * (i - CCH) + h) + P],
                                           start=False, stop=True, skip_group_check=True)
                        if n < NCH - 1:
                            mm.then_inc(B["ymm"], 1)
                mm.then_inc(B["ymm"], 1)
            assert nxt.n == 24
            w("dir", 3)
            pe.matmul(Q[0][:, :], ones_head, Y, start=True, stop=True).then_inc(B["ym"], 1)
            w("rk", 1)
            pe.matmul(Q[2][:, :], ones_head, t3[:, 0:SEQ], start=True, stop=True).then_inc(B["bonus"], 1)
            pe.matmul(Q[3][:, :], lw[:, 2 * P:3 * P], sgd, start=True, stop=True).then_inc(B["gate"], 1)
            w("ysq", 1)
            pe.matmul(Q[1][:, :], ones_head, t1[:, 0:SEQ], start=True, stop=True).then_inc(B["yvar"], 1)

        def pe_attention(t):
            pe = t.eng
            w = lambda n, k: t.wait(C[n], C_PER[n], k)
            nxt = Projection(t, GROUP_C + 1)
            nxt.parts(6)
            w("cp", 1)
            for c in range(10):
                src = vs[:, CTX + P * c:CTX + P * c + P] if c < 8 else vs[:, P * (c - 8):P * (c - 8) + P]
                mm = pe.transpose(Q[c // 4][:, P * (c % 4):P * (c % 4) + P], src, ident)
            mm.then_inc(C["vwp"], 1)
            w("vwe", 1)
            kv = ks[:, lat].rearrange("p (r c) -> p r c", c=GRID_W)

            def scores(x):
                b, h = divmod(x, 2)
                hs = slice(64 * h, 64 * h + 64)
                if x >= 2:
                    w("sadd", x - 1)
                qt = qs[hs, P * b:P * b + P]
                pe.matmul(Q[x % 2][:, 0:256], qt, kv[hs, :, WIN0[b]:WIN0[b] + WC], start=True, stop=True)
                pe.matmul(Q[x % 2][:, 256:512], qt, ks[hs, 0:CTX], start=True, stop=True).then_inc(C["smm"], 1)

            def turn(x):
                w("pn", x + 1)
                if x >= 2:
                    w("tpe", x - 1)
                for c in range(4):
                    mm = pe.transpose(Q[2 + x % 2][:, P * c:P * c + P], PR[x % 2][:, P * c:P * c + P], ident)
                mm.then_inc(C["tp"], 1)

            def values(x):
                b, h = divmod(x, 2)
                w("tpe", x + 1)
                for c in range(4):
                    src = vw[:, 2 * b + c if c < 2 else 6 + c, 64 * h:64 * h + 64]
                    mm = pe.matmul(Q[4][64 * h:64 * h + 64, P * b:P * b + P], src, PT[x % 2][:, c, :],
                                   start=c == 0, stop=c == 3)
                mm.then_inc(C["pv"], 1)

            for x in range(10):
                if x < 8:
                    scores(x)
                    nxt.parts(1)
                if 1 <= x < 9:
                    turn(x - 1)
                    nxt.parts(1)
                if x >= 2:
                    values(x - 2)
            nxt.rest()

        def pe_gmlp(pe):
            t = Turn(pe, 0, tick)
            nxt = Projection(t, GROUP_C + 1 + CPAIRS, 5, 1)

            def turn(j):
                pe.wait_ge(A["gv"], j + 1)
                for n in range(4):
                    mm = pe.transpose(Q[j][:, P * n:P * n + P], gv[j][:, P * n:P * n + P], ident)
                mm.then_inc(A["tp"], 1)

            pe.wait_ge(C["done"], CPAIRS + 1)
            nxt.parts(8)
            for j in range(3):
                turn(j)
            nxt.parts(16)
            turn(3)
            nxt.rest()
            pe.wait_ge(amix_ld, 16)
            for j in range(APAIRS):
                pe.wait_ge(A["ln"], j + 1)
                if j >= 2:
                    pe.wait_ge(A["vch"], j + 1)
                for n in range(4):
                    for h in range(2):
                        g = 2 * j + h
                        mm = pe.matmul(Q[4 + j % 2][64 * h:64 * h + 64, P * n:P * n + P],
                                       vn[j][:, P * n + 64 * h:P * n + 64 * h + 64], amix_s[:, P * g:P * g + P],
                                       start=True, stop=True)
                mm.then_inc(A["mix"], 1)

        def triple(pe, bank, lh, ll, rh, rl, start, stop):
            pe.matmul(bank[:, :], lh, rh, start=start, stop=False)
            pe.matmul(bank[:, :], lh, rl, start=False, stop=False)
            return pe.matmul(bank[:, :], ll, rh, start=False, stop=stop)

        def pe_second_half(pe):
            def gate_row(c):
                for k in range(KT):
                    pe.wait_ge(E["gcb"], KT * c + k + 1)
                    if k >= 2:
                        pe.wait_ge(E["grow"], KT * c + k - 1)
                    pe.matmul(banks[k % 2][:, 0:P], gcb[k % 2], ident, start=True, stop=True).then_inc(E["gmm"], 1)

            gate_row(0)
            pe.wait_ge(E["grow"], KT)
            pe.wait_ge(E["mixl"], KT)
            with pe.Fori(0, 2) as s:
                t = Turn(pe, s, tick)
                for n in range(2):
                    for c in range(KT // 2):
                        pos = 8 * n + c
                        t.wait(split2, 16, pos + 1)
                        for m in range(4):
                            if c == 0:
                                t.wait(E["oev"], 8, 4 * n + m + 1)
                            for k in range(2):
                                mm = triple(pe, banks[4 * n + m], mixh[:, 2 * c + k, P * m:P * m + P],
                                            mixl[:, 2 * c + k, P * m:P * m + P], wh2[pos % 2][:, 512 * k:512 * k + 512],
                                            wl2[pos % 2][:, 512 * k:512 * k + 512], c == 0 and k == 0, c == 7 and k == 1)
                            if c == 7 and m < 3:
                                mm.then_inc(E["omm"], 1)
                        mm.then_inc(used2, 1)
            gate_row(1)
            for k in range(KT):
                for m in range(4):
                    if k == 0:
                        pe.wait_ge(E["ln1"], m + 1)
                    if m == 0 and k >= 2:
                        pe.wait_ge(E["hev"], k - 1)
                    mm = pe.transpose(banks[6 + k % 2][:, P * m:P * m + P], xr[:, m, P * k:P * k + P], ident)
                mm.then_inc(E["htp"], 1)
            pe.wait_ge(E["hsplit"], KT)
            with pe.Fori(0, EFF) as e:
                t = Turn(pe, e, tick)
                w = lambda n, k: t.wait(E[n], E_PER[n], k)
                for f in range(FT):
                    w("urelu", f + PRIME2 - 1)
                    for h in range(2):
                        t.wait(split2, 32, 32 + 2 * f + h + 1)
                        for k in range(8):
                            wk = slice(P * k, P * k + P)
                            mm = triple(pe, banks[f % 2], wh2[h][:, wk], wl2[h][:, wk], hTh[:, 8 * h + k, :],
                                        hTl[:, 8 * h + k, :], h == 0 and k == 0, h == 1 and k == 7)
                        mm.then_inc(used2, 1)
                w("usq", FT + PRIME2)
                for n in range(4):
                    for c in range(FT // 2):
                        pos = 2 * FT + 4 * n + c
                        t.wait(split2, 32, 32 + pos + 1)
                        for m in range(4):
                            if c == 0:
                                w("dev", 4 * n + m + PRIME2 + 1 - 4)
                            for k in range(2):
                                mm = triple(pe, banks[2 + m], hidh[:, 2 * c + k, P * m:P * m + P],
                                            hidl[:, 2 * c + k, P * m:P * m + P], wh2[pos % 2][:, 512 * k:512 * k + 512],
                                            wl2[pos % 2][:, 512 * k:512 * k + 512], c == 0 and k == 0,
                                            c == FT // 2 - 1 and k == 1)
                            if c == FT // 2 - 1 and m < 3:
                                mm.then_inc(E["dmm"], 1)
                        mm.then_inc(used2, 1)

        @block.tensor
        def _(pe):
            pe.wait_ge(setup, 32)
            pe.wait_ge(a_setup, 2)

            def ada_tile(t, b, bank, col, first_loop):
                t.wait(loaded0[b], 16, 16 if first_loop else 16 * (FIRST_ADA // RING0) + 16)
                for k in range(KT):
                    mm = pe.matmul(banks[bank][:, 2 * col:2 * col + 2], ring0k[b][:, k, :], csil[:, k, :],
                                   start=k == 0, stop=k == KT - 1)
                mm.then_inc(used0, 1)

            with pe.Fori(0, FIRST_ADA // RING0) as s:
                t = Turn(pe, s, tick)
                for b in range(RING0):
                    if b in (0, 4):
                        t.wait(mod_ev, 2, 1 + b // 4)
                    ada_tile(t, b, b // 4, b % 4, True)
            pe.wait_ge(cm_ready, 1)
            with pe.Fori(0, CTX_TILES // 2) as s:
                t = Turn(pe, s, tick)
                for b in range(RING0):
                    if b in (0, 3):
                        t.wait(loaded0[b], 16, 16 * (FIRST_ADA // RING0) + 16)
                        t.wait(zst_ev, 2, b // 3 + 1)
                        for k in range(KT):
                            mm = pe.matmul(banks[2 + b // 3][:, 0:CTX], ring0k[b][:, k, :], cm[:, k, :],
                                           start=k == 0, stop=k == KT - 1)
                        mm.then_inc(used0, 1)
                        continue
                    if b in (1, 4):
                        t.wait(mod_ev, 2, 2 * (FIRST_ADA // RING0) + 1 + b // 4)
                    ada_tile(t, b, b // 4, b - 1 if b < 3 else b - 4, False)
            pe.wait_ge(xsplit, 2)
            pe.wait_ge(mod_ev, 2 + 2 * (FIRST_ADA // RING0) + CTX_TILES)
            Projection(Turn(pe, 0, tick), 0).rest()
            Projection(Turn(pe, 0, tick), 1).rest()
            pe.wait_ge(lora_ready, 2)
            with pe.Fori(0, BPAIRS) as j:
                pe_rwkv(Turn(pe, j, tick))
            with pe.Fori(0, CPAIRS) as j:
                pe_attention(Turn(pe, j, tick))
            pe_gmlp(pe)
            pe_second_half(pe)

        def act_take_tile(t, group, q, psum=None):
            if q < 2:
                t.eng.dma_start(zpad[q][:, None, Z_CTX:Z_CTX + CTX],
                                zctxd[bass.ds(2 * (t.j + group) + q, 1)].rearrange("o p n -> p o n")).then_inc(z_ctx, 16)
            act_take_latents(t, group, q)

        def act_take_latents(t, group, q):
            t.wait(used1, 6, 6 * group + 2 * q + 2)
            dst = zpad[q][:, Z_LAT:Z_LAT + SEQ] if q < 2 else zpad[2][:, 1:1 + SEQ]
            nc.scalar.copy(dst, (PA, PB)[q % 2][:, :]).then_inc(z_ev, 1)

        def act_store_mix(t, sems, tile):
            t.wait(sems["done"], 1, 2)
            t.eng.dma_start(mixd[bass.ds(t.j + tile, 1)].rearrange("o p n -> p o n"), mst[:, None, :]).then_inc(mst_out, 16)

        def act_rwkv(t):
            act = t.eng
            w = lambda n, k: t.wait(B[n], B_PER[n], k)
            act.dma_start(lw[:, None, :], loraw[bass.ds(t.j, 1)].rearrange("o p n -> p o n")).then_inc(B["lw"], 16)
            w("convk", 1)
            nc.scalar.activation(t1, cK, ACT.Square, scale=pc[:, 13:14]).then_inc(B["sq"], 1)
            w("tp", 1)
            nc.scalar.copy(VT[:, 0:512], Q[2][:, :])
            nc.scalar.copy(VT[:, 512:TOK], Q[3][:, 0:256]).then_inc(B["tpe"], 1)
            w("ssmax", 2)
            nc.scalar.activation(t2, t3, ACT.Sqrt).then_inc(B["norm"], 1)
            for d in range(2):
                w("dir", d + 1)
                for buf in (LT, RB, GT, RK):
                    a = nc.scalar.copy(buf, zero[:, 0:1].to_broadcast([P, buf.shape[1]]))
                a.then_inc(B["gm0"], 1)
                if d == 0:
                    w("kkn", 1)
                w("lps", 2 * d + 1)
                for n in range(2):
                    a = nc.scalar.activation(t0[:, 384 * n:384 * n + 384], Q[n][:, 0:384], ACT.Tanh, scale=0.5, bias=pch[:, d:d + 1])
                a.then_inc(B["tanh"], 1)
                w("lps", 2 * d + 2)
                for n in range(2):
                    a = nc.scalar.activation(t5[:, 384 * n:384 * n + 384], Q[2 + n][:, 0:384], ACT.Tanh, scale=0.5,
                                             bias=pch[:, 2 + d:3 + d])
                a.then_inc(B["tanh"], 1)
                w("scan", 2 * d + 2)
                inc, exc = ((t2, -CDEC), (t3, -CDEC)) if d == 0 else ((t3, CDEC), (t2, CDEC))
                nc.scalar.activation(t4, exc[0], ACT.Exp, scale=exc[1])
                nc.scalar.activation(t1[:, 0:SEQ], inc[0][:, lat], ACT.Exp, scale=inc[1])
                nc.scalar.activation(t0, inc[0], ACT.Exp, scale=-inc[1])
                nc.scalar.activation(e1, smid, ACT.Exp, scale=-CDEC)
                nc.scalar.activation(e2, sdif, ACT.Exp, scale=-CDEC).then_inc(B["exps"], 1)
                if d == 0:
                    act_take_tile(t, GROUP_B + 1, 0)
                for n, dstt in enumerate((AT, BT, KTT)):
                    w("tp", 3 * d + n + 2)
                    nc.scalar.copy(dstt[:, 0:512], Q[2 * n][:, :])
                    nc.scalar.copy(dstt[:, 512:TOK], Q[2 * n + 1][:, 0:256]).then_inc(B["tpe"], 1)
                idb = ident[:, None, :].to_broadcast([P, 12, P])
                nc.scalar.copy(X.rearrange("p (u n) -> p u n", n=P), idb).then_inc(B["xi"], 1)
                nc.scalar.copy(XT.rearrange("p (u n) -> p u n", n=P), idb).then_inc(B["xi"], 1)
                for g in range(NG):
                    w("gv", 3 * d + g + 1)
                    nc.scalar.copy(TT[:, 256 * g:256 * g + 256], Q[4][:, 0:256]).then_inc(B["gve"], 1)
                w("gve", 3 * d + 3)
                nc.scalar.copy(GVS, TT[:, 0:TOK]).then_inc(B["gvc"], 1)
                w("gvc", d + 1)
                for x in range(6 * NG):
                    g = x % NG
                    w("tmm", 18 * d + x + 1)
                    nc.scalar.copy(TT[:, 512 * g:512 * g + 512], Q[x % 2][:, :]).then_inc(B["tev"], 1)
                w("zw", d + 1)
                nc.scalar.copy(ZS[:, 0:512], Q[0][:, :])
                nc.scalar.copy(ZS[:, 512:TOK], Q[1][:, 0:256]).then_inc(B["zwe"], 1)
                nc.scalar.copy(WT[:, 0:512], Q[2][:, :])
                nc.scalar.copy(WT[:, 512:TOK], Q[3][:, 0:256]).then_inc(B["zwe"], 1)
                act_take_tile(t, GROUP_B + 1, d + 1)
            w("yc", 1)
            nc.scalar.activation(t1[:, 0:SEQ], t0[:, 0:SEQ], ACT.Square).then_inc(B["ysq"], 1)
            w("yvar", 1)
            nc.scalar.activation(t2[:, 0:SEQ], Q[1][:, :], ACT.Sqrt, scale=1.0 / HD, bias=eps_gn).then_inc(B["ystd"], 1)
            act_store_mix(t, B, APAIRS)

        def act_attention(t):
            act = t.eng
            w = lambda n, k: t.wait(C[n], C_PER[n], k)
            act.dma_start(bias_s.rearrange("p t h n -> p (t h n)")[:, None, :],
                          bias[bass.ds(t.j, 1)].rearrange("o p n -> p o n")).then_inc(C["bias"], 16)
            t.wait(z_ev, 3, 3 * GROUP_C + 3)
            t.wait(z_ctx, 32, 32 * (GROUP_C + 1))
            rows = zpad[1][:, Z_LAT:Z_LAT + SEQ].rearrange("p (r c) -> p r c", c=GRID_W)
            nc.scalar.copy(ks[:, 0:CTX], zpad[0][:, Z_CTX:Z_CTX + CTX])
            nc.scalar.copy(ks[:, lat], zpad[0][:, Z_LAT:Z_LAT + SEQ])
            nc.scalar.copy(vs[:, 0:CTX], zpad[1][:, Z_CTX:Z_CTX + CTX])
            for b in range(4):
                nc.scalar.copy(vs[:, CTX + 256 * b:CTX + 256 * b + 256].rearrange("p (r c) -> p r c", c=WC),
                               rows[:, :, WIN0[b]:WIN0[b] + WC])
            nc.scalar.activation(qs.rearrange("p (b r c) -> p r b c", b=4, c=QC),
                                 zpad[2][:, 1:1 + SEQ].rearrange("p (r b c) -> p r b c", b=4, c=QC), ACT.Copy,
                                 scale=HD ** -0.5).then_inc(C["cp"], 1)
            w("cp", 1)
            w("vwp", 1)
            for c in range(3):
                a = nc.scalar.copy(vw[:, 4 * c:min(4 * c + 4, 10), :],
                                   Q[c][:, 0:P * min(4, 10 - 4 * c)].rearrange("p (c n) -> p c n", n=P))
            a.then_inc(C["vwe"], 1)

            def expo(x):
                w("max", x + 1)
                if x >= 2:
                    w("tp", x - 1)
                nc.scalar.activation(PR[x % 2], S[x % 2], ACT.Exp, bias=negmax[:, x:x + 1],
                                     accum_out=esum[:, x:x + 1]).then_inc(C["exp"], 1)

            def turned(x):
                w("tp", x + 1)
                if x >= 2:
                    w("pv", x - 1)
                nc.scalar.copy(PT[x % 2].rearrange("p c q -> p (c q)"), Q[2 + x % 2][:, :]).then_inc(C["tpe"], 1)

            for x in range(9):
                if x < 8:
                    expo(x)
                if x >= 1:
                    turned(x - 1)
                if x in (2, 6):
                    act_take_tile(t, GROUP_C + 1, x // 4)
            act_take_latents(t, GROUP_C + 1, 2)
            act_store_mix(t, C, APAIRS + BPAIRS)

        def act_gmlp(act):
            group = GROUP_C + CPAIRS
            for j in range(3):
                src = zpad[j][:, Z_LAT:Z_LAT + SEQ] if j < 2 else zpad[2][:, 1:1 + SEQ]
                act.wait_ge(z_ev, 3 * group + j + 1)
                nc.scalar.activation(gv[j], src, ACT.Gelu_apprx_tanh).then_inc(A["gv"], 1)
            for q in range(5):
                bank = (PB, PA)[q % 2]
                act.wait_ge(used1, 6 * (group + 1) + 2 * q + 2)
                nc.scalar.activation(gu[q - 1] if q else gv[3], bank[:, :], ACT.Gelu_apprx_tanh).then_inc(z_ev, 1)
                if q == 0:
                    act.wait_ge(z_ev, 3 * (group + 1) + 1)
                    nc.scalar.copy(vt[3], gv[3]).then_inc(A["gv"], 1)
                    for j in range(3):
                        act.wait_ge(A["tp"], j + 1)
                        nc.scalar.copy(vt[j], Q[j][:, :]).then_inc(A["tpe"], 1)
                if q == 3:
                    act.wait_ge(A["tp"], 4)
                    nc.scalar.copy(vt[3], Q[3][:, :]).then_inc(A["tpe"], 1)
            act.wait_ge(A["var"], 1)
            nc.scalar.activation(ars, amv.rearrange("p (u s) -> p u s", s=2)[:, :, 1], ACT.Sqrt, bias=eps_ln).then_inc(A["std"], 1)
            for j in range(APAIRS):
                act.wait_ge(A["done"], j + 1)
                act.dma_start(mixd[j], gout[j]).then_inc(mix_out, 16)

        def act_second_half(act):
            act.wait_ge(A["done"], APAIRS)

            def high_part(t, pos, per, base):
                t.wait(rawld2[pos % RING2], 16 * per // RING2, 16 * ((base + pos) // RING2) + 16)
                if base + pos >= SPLIT2:
                    t.wait(used2, per, base + pos + 1 - SPLIT2)
                nc.scalar.copy(wh2[pos % SPLIT2], raw2[pos % RING2]).then_inc(high2, 1)

            def gate_row(c):
                for k in range(KT):
                    act.wait_ge(E["gmm"], KT * c + k + 1)
                    if c and k == 0:
                        act.wait_ge(E["oev"], 8 + 16)
                    nc.scalar.copy(grow[:, P * k:P * k + P], banks[k % 2][:, 0:P]).then_inc(E["grow"], 1)

            def std(c):
                for m in range(4):
                    act.wait_ge(E["var"], 4 * c + m + 1)
                    nc.scalar.activation(rs2[:, m:m + 1], mv2[:, m, 1:2], ACT.Sqrt, bias=eps_ln).then_inc(E["std"], 1)

            once = Turn(act, 0, tick)
            high_part(once, 0, 32, 0)
            high_part(once, 1, 32, 0)
            act.wait_ge(E["mixraw"], 16)
            for k in range(KT):
                nc.scalar.copy(mixh[:, k, :], mixraw[:, k, :]).then_inc(E["mixh"], 1)
            gate_row(0)
            for pos in range(2, 2 * KT):
                high_part(once, pos, 32, 0)
            gate_row(1)
            std(0)
            for k in range(KT):
                act.wait_ge(E["htp"], k + 1)
                if k >= 2:
                    act.wait_ge(E["hsplit"], k - 1)
                nc.scalar.activation(etmp[k % 2], banks[6 + k % 2][:, :], ACT.Identity, scale=scl2[:, k:k + 1],
                                     bias=modv[:, 3, k, 0:1]).then_inc(E["hev"], 1)
            with act.Fori(0, EFF) as e:
                t = Turn(act, e, tick)
                high_part(t, 0, 32, 32)
                high_part(t, 1, 32, 32)
                for f in range(FT):
                    high_part(t, 2 * f + 2, 32, 32)
                    high_part(t, 2 * f + 3, 32, 32)
                    t.wait(used2, 32, 32 + 2 * f + 2)
                    t.wait(E["usq"], FT, f + PRIME2 - 1)
                    nc.scalar.activation(etmp[f % 2], banks[f % 2][:, :], ACT.Relu).then_inc(E["urelu"], 1)
                for pos in range(2 * FT + 2, 4 * FT):
                    high_part(t, pos, 32, 32)
            std(1)

        @block.scalar
        def _(act):
            act.wait_ge(setup, 32)
            nc.scalar.activation(cth, cin, ACT.Tanh, scale=0.5).then_inc(a_setup, 1)
            act.wait_ge(v_mod, 2)
            act.wait_ge(setc, 16)
            for k in range(KT):
                a = nc.scalar.activation(cm[:, k, :], cm[:, k, :], ACT.Identity, scale=scl1[:, k, 1:2], bias=modv[:, 0, k, 1:2])
            a.then_inc(cm_ready, 1)
            with act.Fori(0, CTX_TILES // 2) as s:
                t = Turn(act, s, tick)
                for n in range(2):
                    t.wait(used0, RING0, FIRST_ADA + 3 * n + 1)
                    t.wait(zst_out[n], 16, 16)
                    nc.scalar.copy(zst[n], banks[2 + n][:, 0:CTX]).then_inc(zst_ev, 1)
                    t.wait(zst_ev, 2, 2 + n + 1)
                    act.dma_start(zctxd[bass.ds(s * 2 + n, 1)].rearrange("o p n -> p o n"), zst[n][:, None, :]
                                  ).then_inc(zst_out[n], 16)
            for n in range(2):
                act.dma_start(zctxd[CTX_TILES + n], zst[n]).then_inc(zst_out[n], 16)
            for n in range(2):
                act.wait_ge(zst_out[n], 16 * (CTX_TILES // 2 + 2))
            act.wait_ge(used0, N0)
            act.dma_start(small3, small["b"]).then_inc(bparams, 16)
            act.wait_ge(zeroed, 3)
            t = Turn(act, 0, tick)
            for q in range(3):
                if q < 2:
                    act.dma_start(zpad[q][:, Z_CTX:Z_CTX + CTX], zctxd[q]).then_inc(z_ctx, 16)
                act_take_latents(t, 0, q)
            act.wait_ge(lora_v, 3)
            nc.scalar.activation(tw, tw, ACT.Tanh).then_inc(lora_ready, 1)
            nc.scalar.activation(sgd, sgd, ACT.Tanh, scale=0.5).then_inc(a_setup, 1)
            for q in range(3):
                if q < 2:
                    act.dma_start(zpad[q][:, Z_CTX:Z_CTX + CTX], zctxd[2 + q]).then_inc(z_ctx, 16)
                act_take_latents(t, 1, q)
            with act.Fori(0, BPAIRS) as j:
                act_rwkv(Turn(act, j, tick))
            act.dma_start(cmask_s, small["cmask"]).then_inc(cmask_ld, 16)
            act.dma_start(amix_s, small["amix"]).then_inc(amix_ld, 16)
            with act.Fori(0, CPAIRS) as j:
                act_attention(Turn(act, j, tick))
            act_gmlp(act)
            act_second_half(act)

        def dve_rwkv(t, conv):
            V = nc.vector
            dve = t.eng
            w = lambda n, k: t.wait(B[n], B_PER[n], k)
            t.step(V.tensor_copy(pc[:, None, :], parall.rearrange("p (j n) -> p j n", n=NPAR)[:, bass.ds(t.j, 1), :]))
            V.tensor_scalar(pch[:, 0:4], pc[:, 9:13], 0.5, None, ALU.mult)
            V.tensor_scalar(pch[:, 4:5], pc[:, 14:15], 0.5, None, ALU.mult)
            t.step(V.tensor_scalar(pch[:, 5:6], pc[:, 14:15], -0.5, 1.0, ALU.mult, ALU.add))
            t.wait(z_ctx, 32, 32 * (GROUP_B + 1))
            t.wait(z_ev, 3, 3 * GROUP_B + 1)
            conv(t.step, zpad[0], pc[:, 0:3], cK, False, B["convk"], TT)
            w("convk", 1)
            t.wait(z_ev, 3, 3 * GROUP_B + 2)
            conv(t.step, zpad[1], pc[:, 3:6], cV, False, B["convv"], X)
            w("convv", 1)
            t.wait(z_ev, 3, 3 * GROUP_B + 3)
            conv(t.step, zpad[2], pc[:, 6:9], cR, True, B["convr"], XT)
            w("convr", 1)
            w("ss", 1)
            V.tensor_scalar(t3[:, 0:384], Q[0][:, 0:384], 1e-12, None, ALU.max).then_inc(B["ssmax"], 1)
            V.tensor_scalar(t3[:, 384:TOK], Q[1][:, 0:384], 1e-12, None, ALU.max).then_inc(B["ssmax"], 1)
            w("norm", 1)
            t.step(V.reciprocal(t4, t2))
            V.scalar_tensor_tensor(KKN, cK, pc[:, 13:14], t4, ALU.mult, ALU.mult).then_inc(B["kkn"], 1)
            w("kkn", 1)
            for d in range(2):
                w("tanh", 2 * d + 1)
                t.step(V.tensor_scalar(t0, t0, 1.0, None, ALU.add))
                for i in range(NCH):
                    a = V.tensor_tensor_scan(t1[:, tokc(i)], ones_row, t0[:, tokc(i)], 0.0, ALU.mult, ALU.add)
                t.step(a)
                t1v = t1.rearrange("p (i n) -> p i n", n=P)
                t.step(V.tensor_copy(smid[:, :, None], t1v[:, :, 63:64]))
                V.tensor_tensor(sdif[:, :, None], t1v[:, :, 127:128], smid[:, :, None], ALU.subtract).then_inc(B["scan"], 1)
                t.step(V.tensor_tensor(t2.rearrange("p (i n) -> p i n", n=P), t1v, smid[:, :, None].to_broadcast([P, NCH, P]),
                                       ALU.subtract))
                V.tensor_tensor(t3, t2, t0, ALU.subtract).then_inc(B["scan"], 1)
                w("exps", d + 1)
                w("tanh", 2 * d + 2)
                t.step(V.tensor_scalar(t2, t5, pch[:, 4:5], pch[:, 5:6], ALU.mult, ALU.add))
                t.step(V.tensor_tensor(t2, t2, cK, ALU.mult))
                if d == 0:
                    V.tensor_copy(KS, t2[:, lat])
                else:
                    V.tensor_tensor(KS, KS, t2[:, lat], ALU.add)
                V.tensor_tensor(KH, t2, t0, ALU.mult)
                t.step(V.scalar_tensor_tensor(t3, t5, 1.0, KKN, ALU.add, ALU.mult))
                V.scalar_tensor_tensor(BH, t3, 0.5, t0, ALU.mult, ALU.mult)
                V.scalar_tensor_tensor(AH, KKN, -1.0, t4, ALU.mult, ALU.mult)
                V.tensor_tensor(RH, cR, t1[:, 0:SEQ], ALU.mult).then_inc(B["hats"], 1)
                pre, post = (e1, e2) if d == 0 else (e2, e1)
                t.step(V.tensor_copy(pp, e1))
                for n in range(NCH - 1):
                    a, b = ORDER[d][n], ORDER[d][n + 1]
                    ins = V.tensor_tensor(pp[:, a:a + 1], post[:, a:a + 1], pre[:, b:b + 1], ALU.mult)
                t.step(ins)
                w("gm0", d + 1)
                w("xi", 2 * d + 2)
                sm, im = gmask[:, d, 0, :].bitcast(U32), gmask[:, d, 1, :].bitcast(U32)
                bc = lambda m, k: m[:, None, :].to_broadcast([P, k, P])
                m1, m1T = lmask[:, 0, d, :].bitcast(U32), lmask[:, 0, 1 - d, :].bitcast(U32)
                for g in range(NG):
                    w("gram", 3 * d + g + 1)
                    if g:
                        w("gv", 3 * d + g)
                    for h in range(2):
                        two = lambda bank, c: bank[:, c:c + 256].rearrange("p (i n) -> p i n", n=P)
                        i2 = slice(2 * g, 2 * g + 2)
                        V.copy_predicated(units(LT)[:, i2, h, :], bc(sm, 2), two(Q[h], 0))
                        V.copy_predicated(units(XT)[:, i2, h, :], bc(m1T, 2), two(Q[h], 0))
                        V.copy_predicated(units(X)[:, i2, h, :], bc(m1, 2), two(Q[4 + h], 0))
                        ins = V.copy_predicated(units(GT)[:, :, h, :], bc(sm, 2), two(Q[2 + h], 0))
                        if g:
                            V.copy_predicated(units(RB)[:, 2 * g - 2:2 * g, h, :], bc(im, 2), two(Q[h], 256))
                            ins = V.copy_predicated(units(RK)[:, :, h, :], bc(im, 2), two(Q[2 + h], 256))
                    ins.then_inc(B["gramev"], 1)
                    if g:
                        w("gv", 3 * d + g + 1)
                        ys = Y[:, 256 * (g - 1):256 * g]
                        if d == 0:
                            V.tensor_copy(ys, Q[5][:, 0:256]).then_inc(B["yk"], 1)
                        else:
                            V.tensor_tensor(ys, Q[5][:, 0:256], ys, ALU.add).then_inc(B["yk"], 1)
                for x in range(6 * NG):
                    l, g = divmod(x, NG)
                    four = lambda a: a.rearrange("p (u n) -> p u n", n=P)
                    mX, mT = lmask[:, l + 1, d, :].bitcast(U32), lmask[:, l + 1, 1 - d, :].bitcast(U32)
                    w("dmm", 18 * d + x + 1)
                    if l < 5:
                        V.copy_predicated(four(X[:, 512 * g:512 * g + 512]), bc(mX, 4), four(Q[2 + x % 2][:, :]))
                    V.copy_predicated(four(XT[:, 512 * g:512 * g + 512]), bc(mT, 4), four(Q[4 + x % 2][:, :])).then_inc(B["dev"], 1)
                w("zw", d + 1)
                V.tensor_tensor(NK.rearrange("p (i n) -> p i n", n=HD), Q[4][:, 0:384].rearrange("p (i n) -> p i n", n=HD),
                                pp[:, :, None].to_broadcast([P, NCH, HD]), ALU.mult).then_inc(B["zwe"], 1)
                w("zwe", 3 * d + 3)
                for n, i in enumerate(ORDER[d]):
                    cur, nxt = MB[n % 2], MB[(n + 1) % 2]
                    if n:
                        w("umm", 5 * d + n)
                        V.tensor_tensor(US, Q[0][:, 0:P], ZS[:, tokc(i)], ALU.add).then_inc(B["uev"], 1)
                    if n < NCH - 1:
                        if n:
                            for h in range(2):
                                hs = slice(64 * h, 64 * h + 64)
                                ins = V.scalar_tensor_tensor(MQ[hs, :], cur[hs, hs], pp[hs, i:i + 1], NK[hs, HD * i:HD * i + HD],
                                                             ALU.mult, ALU.add)
                            t.step(ins)
                        w("mmm", 5 * d + n + 1)
                        for h in range(2):
                            hs = slice(64 * h, 64 * h + 64)
                            add = MQ[hs, :] if n else NK[hs, HD * i:HD * i + HD]
                            ins = V.scalar_tensor_tensor(nxt[hs, hs], Q[1][hs, 0:HD], pp[hs, i:i + 1], add, ALU.mult, ALU.add)
                        ins.then_inc(B["mev"], 1)
                w("ymm", 4 * d + 4)
                V.tensor_tensor(Y, Q[5][:, :], Y, ALU.add).then_inc(B["dir"], 1)
                w("dir", d + 2)
            V.scalar_tensor_tensor(t3[:, 0:SEQ], cR, pc[:, 15:16], KS, ALU.mult, ALU.mult).then_inc(B["rk"], 1)
            w("ym", 1)
            V.scalar_tensor_tensor(t0[:, 0:SEQ], Q[0][:, :], -1.0 / HD, Y, ALU.mult, ALU.add).then_inc(B["yc"], 1)
            w("yc", 1)
            w("bonus", 1)
            t.step(V.tensor_tensor(t4[:, 0:SEQ], Q[2][:, :], cV[:, lat], ALU.mult))
            w("ystd", 1)
            t.step(V.reciprocal(t5[:, 0:SEQ], t2[:, 0:SEQ]))
            t.step(V.tensor_tensor(t0[:, 0:SEQ], t0[:, 0:SEQ], t5[:, 0:SEQ], ALU.mult))
            t.step(V.tensor_scalar(t0[:, 0:SEQ], t0[:, 0:SEQ], pc[:, 16:17], pc[:, 17:18], ALU.mult, ALU.add))
            t.step(V.tensor_tensor(t0[:, 0:SEQ], t0[:, 0:SEQ], t4[:, 0:SEQ], ALU.add))
            w("gate", 1)
            t.wait(mst_out, 16, 16)
            V.tensor_tensor(mst, Q[3][:, :], t0[:, 0:SEQ], ALU.mult).then_inc(B["done"], 1)
            assert t.n == t.per, ("b", t.n)

        def dve_attention(t):
            V = nc.vector
            w = lambda n, k: t.wait(C[n], C_PER[n], k)
            w("bias", 16)
            t.step(V.tensor_tensor(bias_s, bias_s, cmask_s.rearrange("p (t o n) -> p t o n", t=4, o=1).to_broadcast([P, 4, 2, 256]),
                                   ALU.add))

            def addmax(x):
                b, h = divmod(x, 2)
                w("smm", x + 1)
                if x >= 2:
                    w("exp", x - 1)
                V.tensor_copy(S[x % 2][:, 256:512], Q[x % 2][:, 256:512])
                ins = V.tensor_tensor(S[x % 2][:, 0:256], Q[x % 2][:, 0:256], bias_s[:, b, h, :], ALU.add)
                ins.then_inc(C["sadd"], 1)
                w("sadd", x + 1)
                V.tensor_reduce(negmax[:, x:x + 1], S[x % 2], AX.X, ALU.max, negate=True).then_inc(C["max"], 1)

            def norm(x):
                w("exp", x + 1)
                t.step(V.reciprocal(erec[:, x:x + 1], esum[:, x:x + 1]))
                V.tensor_scalar(PR[x % 2], PR[x % 2], erec[:, x:x + 1], None, ALU.mult).then_inc(C["pn"], 1)

            for x in range(9):
                if x < 8:
                    addmax(x)
                if x >= 1:
                    norm(x - 1)
            w("pv", 8)
            t.wait(mst_out, 16, 16 * (BPAIRS + 1))
            ins = V.tensor_copy(mst.rearrange("p (r b c) -> p b r c", b=4, c=QC),
                                Q[4][:, :].rearrange("p (b r c) -> p b r c", b=4, c=QC))
            ins.then_inc(C["done"], 1)
            assert t.n == t.per, ("c", t.n)

        def dve_gmlp(dve):
            V = nc.vector
            for j in range(APAIRS):
                dve.wait_ge(A["tpe"], j + 1)
                for u in range(8):
                    V.bn_stats(ast[:, 48 * j + 6 * u:48 * j + 6 * u + 6], vt[j][:, HD * u:HD * u + HD])
            V.tensor_copy(ars[:, 0:1], eps_ln).then_inc(A["vch"], 1)
            dve.wait_ge(A["vch"], 1)
            for u in range(32):
                ins = V.bn_aggr(amv[:, 2 * u:2 * u + 2], ast[:, 6 * u:6 * u + 6])
            ins.then_inc(A["var"], 1)
            dve.wait_ge(A["std"], 1)
            V.reciprocal(ars, ars).then_inc(A["vch"], 1)
            dve.wait_ge(A["vch"], 2)
            for j in range(APAIRS):
                for u in range(8):
                    v = 8 * j + u
                    ins = V.tensor_scalar(vn[j][:, HD * u:HD * u + HD], vt[j][:, HD * u:HD * u + HD], amv[:, 2 * v:2 * v + 1],
                                          ars[:, v:v + 1], ALU.subtract, ALU.mult)
                ins.then_inc(A["ln"], 1)
            for j in range(APAIRS):
                dve.wait_ge(A["mix"], j + 1)
                dve.wait_ge(z_ev, 3 * (GROUP_C + CPAIRS + 1) + 2 + j)
                V.tensor_tensor(gout[j].rearrange("p (n i) -> p n i", n=4), Q[4 + j % 2][:, :].rearrange("p (n i) -> p n i", n=4),
                                agb_s[:, None, P * j:P * j + P].to_broadcast([P, 4, P]), ALU.add).then_inc(A["vch"], 1)
                dve.wait_ge(A["vch"], 3 + j)
                V.tensor_tensor(gout[j], gout[j], gu[j], ALU.mult).then_inc(A["done"], 1)

        def dve_second_half(dve):
            V = nc.vector
            n_v = [0]

            def step(ins):
                n_v[0] += 1
                ins.then_inc(E["vch"], 1)
                dve.wait_ge(E["vch"], n_v[0])

            dve.wait_ge(A["done"], APAIRS)

            def gate_cols(c):
                for k in range(KT):
                    if k >= 2 or c:
                        dve.wait_ge(E["gmm"], KT * c + k - 1)
                    V.tensor_copy(gcb[k % 2], modv[:, 2 + 3 * c, k, 0:1].to_broadcast([P, P])).then_inc(E["gcb"], 1)

            gate_cols(0)
            for k in range(KT):
                dve.wait_ge(E["mixh"], k + 1)
                V.tensor_tensor(mixl[:, k, :], mixraw[:, k, :], mixh[:, k, :].bitcast(F32), ALU.subtract).then_inc(E["mixl"], 1)
            dve.wait_ge(E["grow"], KT)
            dve.wait_ge(E["x"], 16)
            with dve.Fori(0, 2) as s:
                t = Turn(dve, s, tick, E["och"], E_PER["och"])
                for n in range(2):
                    for m in range(4):
                        if m < 3:
                            t.wait(E["omm"], 6, 3 * n + m + 1)
                        else:
                            t.wait(used2, 16, 8 * n + 8)
                        cols = bass.ds(s * 1024 + 512 * n, 512)
                        V.tensor_tensor(etmp[m % 2], banks[4 * n + m][:, :], grow[:, cols], ALU.mult).then_inc(E["oev"], 1)
                        t.wait(E["oev"], 8, 8 + 4 * n + m + 1)
                        t.step(V.scalar_tensor_tensor(xr[:, m, cols], xr[:, m, cols], ALPHA, etmp[m % 2], ALU.mult, ALU.add))
                        t.step(V.bn_stats(st2[:, m, bass.ds(s * 12 + 6 * n, 6)], xr[:, m, cols]))
            assert t.n == t.per

            gate_cols(1)

            def norm(c, sems):
                for m in range(4):
                    V.bn_aggr(mv2[:, m, :], st2[:, m, :]).then_inc(E["var"], 1)
                for m in range(4):
                    dve.wait_ge(E["std"], 4 * c + m + 1)
                    step(V.reciprocal(rs2[:, m:m + 1], rs2[:, m:m + 1]))
                    step(V.tensor_scalar(xr[:, m, :], xr[:, m, :], mv2[:, m, 0:1], rs2[:, m:m + 1], ALU.subtract, ALU.mult))
                    step(V.tensor_tensor(xr[:, m, :], xr[:, m, :], lng, ALU.mult))
                    V.tensor_tensor(xr[:, m, :], xr[:, m, :], lnb, ALU.add).then_inc(sems, 1)
                dve.wait_ge(sems, 4)

            dve.wait_ge(E["ln"], 32)
            norm(0, E["ln1"])
            for k in range(KT):
                dve.wait_ge(E["hev"], k + 1)
                V.tensor_copy(hTh[:, k, :], etmp[k % 2]).then_inc(E["hch"], 1)
                dve.wait_ge(E["hch"], k + 1)
                V.tensor_tensor(hTl[:, k, :], etmp[k % 2], hTh[:, k, :].bitcast(F32), ALU.subtract).then_inc(E["hsplit"], 1)
            dve.wait_ge(E["htp"], KT)
            for m in range(4):
                ins = V.tensor_scalar(xr[:, m, :], xr[:, m, :], ALPHA, None, ALU.mult)
            step(ins)
            dve.wait_ge(E["grow"], 2 * KT)
            with dve.Fori(0, EFF) as e:
                t = Turn(dve, e, tick, E["qch"], E_PER["qch"])
                w = lambda n, k: t.wait(E[n], E_PER[n], k)
                t.wait(used2, 32, 32)
                for f in range(FT):
                    w("urelu", f + 1 + PRIME2)
                    V.tensor_tensor(etmp[f % 2], etmp[f % 2], etmp[f % 2], ALU.mult).then_inc(E["uch"], 1)
                    w("uch", 2 * f + 1)
                    V.tensor_copy(hidh[:, f, :], etmp[f % 2]).then_inc(E["uch"], 1)
                    w("uch", 2 * f + 2)
                    V.tensor_tensor(hidl[:, f, :], etmp[f % 2], hidh[:, f, :].bitcast(F32), ALU.subtract).then_inc(E["usq"], 1)
                for n in range(4):
                    cols = slice(512 * n, 512 * n + 512)
                    for m in range(4):
                        if m < 3:
                            w("dmm", 3 * n + m + 1)
                        else:
                            t.wait(used2, 32, 32 + 2 * FT + 4 * n + 4)
                        V.tensor_tensor(dtmp[m % 2], banks[2 + m][:, :], grow[:, cols], ALU.mult).then_inc(E["dev"], 1)
                        w("dev", 4 * n + m + 1 + PRIME2)
                        t.step(V.tensor_tensor(xr[:, m, cols], xr[:, m, cols], dtmp[m % 2], ALU.add))
            for n in range(4):
                for m in range(4):
                    ins = V.bn_stats(st2[:, m, 6 * n:6 * n + 6], xr[:, m, 512 * n:512 * n + 512])
            step(ins)
            dve.wait_ge(E["ln2row"], 32)
            norm(1, E["fin"])


        @block.vector
        def _(dve):
            V = nc.vector
            n_v = [0]

            def step(ins):
                n_v[0] += 1
                ins.then_inc(v_setup, 1)
                dve.wait_ge(v_setup, n_v[0])

            step(V.memset(eps_ln, 1e-5))
            step(V.memset(eps_gn, 64e-5))
            step(V.memset(zero, 0.0))
            for s, n in ((B["done"], 1), (B["dir"], 1), (C["done"], 1), (mod_ev, 2), (zst_ev, 2), (zst_out[0], 16), (zst_out[1], 16), (mst_out, 16),
                         (E["oev"], 8), (E["urelu"], PRIME2), (E["dev"], PRIME2), (E["usq"], PRIME2)):
                dve.sem_inc(s, n)
            dve.wait_ge(setup, 32)
            dve.wait_ge(a_setup, 1)
            step(V.tensor_scalar(cth, cth, 1.0, 0.5, ALU.add, ALU.mult))
            V.tensor_tensor(csil.rearrange("p k s -> p (k s)"), cth, cin, ALU.mult).then_inc(a_setup, 1)

            def modulation(s, per, base, parts):
                for bank, tile0, count, used in parts:
                    dve.wait_ge(used0, s * RING0 + used)
                    dve.sem_inc(tick, 1)
                    at = bass.ds(s * per + (base + tile0), count)
                    V.tensor_tensor(mod.rearrange("p (t s) -> p t s", s=2)[:, at, :],
                                    banks[bank][:, 0:2 * count].rearrange("p (t s) -> p t s", s=2),
                                    adab_s[:, :, None][:, at, :].to_broadcast([P, count, 2]), ALU.add).then_inc(mod_ev, 1)

            with dve.Fori(0, FIRST_ADA // RING0) as s:
                modulation(s, RING0, 0, ((0, 0, 4, 4), (1, 4, 3, 7)))
            dve.wait_ge(mod_ev, 2 + 2 * (FIRST_ADA // RING0))
            V.tensor_scalar_add(scl1[:, :, :], modv[:, 1, :, :], 1.0).then_inc(v_mod, 1)
            dve.wait_ge(v_mod, 1)
            V.tensor_copy(zero, zero).then_inc(v_mod, 1)
            with dve.Fori(0, CTX_TILES // 2) as s:
                modulation(s, 5, FIRST_ADA, ((0, 0, 2, FIRST_ADA + 3), (1, 2, 3, FIRST_ADA + 7)))
            dve.wait_ge(mod_ev, 2 + 2 * (FIRST_ADA // RING0) + CTX_TILES)
            step(V.tensor_scalar_add(scl2, modv[:, 4, :, 0], 1.0))
            for n in range(2):
                dve.wait_ge(zst_out[n], 16 * (CTX_TILES // 2 + 2))
            dve.wait_ge(used0, N0)
            dve.wait_ge(xsplit, 2)
            for z in zpad:
                V.memset(z, 0.0).then_inc(zeroed, 1)
            for z in MB:
                V.memset(z, 0.0).then_inc(zeroed, 1)
            dve.wait_ge(bparams, 16)

            def conv(step, z, taps, dst, lat_only, last, tmp):
                n = SEQ if lat_only else TOK + 2
                step(V.tensor_scalar(tmp[:, 0:n], z[:, 0:n], taps[:, 0:1], None, ALU.mult))
                step(V.scalar_tensor_tensor(tmp[:, 0:n], z[:, 1:1 + n], taps[:, 1:2], tmp[:, 0:n], ALU.mult, ALU.add))
                if lat_only:
                    V.scalar_tensor_tensor(dst, z[:, 2:2 + n], taps[:, 2:3], tmp[:, 0:n], ALU.mult, ALU.add).then_inc(last, 1)
                else:
                    V.scalar_tensor_tensor(dst[:, 0:CTX], z[:, 2:2 + CTX], taps[:, 2:3], tmp[:, 0:CTX], ALU.mult, ALU.add)
                    V.scalar_tensor_tensor(dst[:, lat], z[:, 4 + CTX:4 + TOK], taps[:, 2:3], tmp[:, CTX + 2:TOK + 2],
                                           ALU.mult, ALU.add).then_inc(last, 1)

            for n, dst in enumerate((tw, ta, sgd)):
                dve.wait_ge(z_ev, n + 1)
                if n < 2:
                    dve.wait_ge(z_ctx, 32)
                conv(step, zpad[n], lp[:, 3 * n:3 * n + 3], dst, n == 2, lora_v, TT)
                dve.wait_ge(lora_v, n + 1)
            dve.wait_ge(a_setup, 3)
            V.tensor_scalar(sgd, sgd, 1.0, 0.5, ALU.add, ALU.mult).then_inc(lora_ready, 1)
            dve.wait_ge(zeroed, 5)
            dve.wait_ge(lora_ready, 2)
            with dve.Fori(0, BPAIRS) as j:
                dve_rwkv(Turn(dve, j, tick, B["vch"], B_PER["vch"]), conv)
            dve.wait_ge(cmask_ld, 16)
            with dve.Fori(0, CPAIRS) as j:
                dve_attention(Turn(dve, j, tick, C["vch"], C_PER["vch"]))
            dve_gmlp(dve)
            dve_second_half(dve)

def tiles(w):
    r, c = w.shape
    return w.reshape(r // P, P, c // P, P).transpose(2, 1, 0, 3).reshape(c // P, P, r)


def wide_tiles(w):
    r, c = w.shape
    return w.reshape(r // 256, 2, P, c // 512, 512).transpose(3, 0, 2, 1, 4).reshape(-1, P, HALF)


def window_masks():
    m = np.zeros((P, 4, ROWS, WC), np.float32)
    for b in range(4):
        for c in range(QC):
            col = QC * b + c
            start = min(max(col - 8, 0), GRID_W - 16)
            keys = WIN0[b] + np.arange(WC)
            m[c::QC, b, :, :] = np.where((keys >= start) & (keys < start + 16), 0.0, -1e30)
    return m.reshape(P, 4 * 256)


def triangles():
    p, f = np.arange(P)[:, None], np.arange(P)[None, :]
    g = np.stack([f > p, f >= p, f < p, f <= p], 1)
    out = [g.reshape(P, 512)]
    for m in [1] + LEVELS:
        out += [(p // m % 2 == 1) & (f // m == p // m - 1), (f // m % 2 == 1) & (p // m == f // m - 1)]
    return np.concatenate([np.asarray(a, np.float32) for a in out], 1)


def kernel(**inputs):
    import concourse.bacc as bacc
    from concourse.bass_utils import run_bass_kernel_spmd

    a = {k: np.asarray(v) for k, v in inputs.items()}
    f = np.ascontiguousarray
    win = tiles(a["w_in"][0])
    b0 = 2 * 512 // P
    c0 = b0 + 21
    col = lambda v, n: v.reshape(n, P)
    halves = lambda w: w.reshape(-1, P, 2, HALF).transpose(0, 2, 1, 3).reshape(-1, P, HALF)
    order = [b0 + 18, b0 + 19, b0 + 20]
    ctx_order = [b0 + 18, b0 + 19]
    for j in range(BPAIRS):
        order += [b0 + 6 + j, b0 + 12 + j, b0 + j]
        ctx_order += [b0 + 6 + j, b0 + 12 + j]
    for j in range(CPAIRS):
        order += [c0 + 6 + j, c0 + 12 + j, c0 + j]
        ctx_order += [c0 + 6 + j, c0 + 12 + j]
    order += [4, 5, 6, 7, 0, 1, 2, 3]
    stream1 = halves(win[order])
    ada = np.concatenate([tiles(a["ada_w"][0]), np.zeros((PAD_ADA - ADA_TILES, P, TILE), np.float32)])
    parts = [ada[0:FIRST_ADA]]
    for s in range(CTX_TILES // 2):
        n = FIRST_ADA + 5 * s
        parts += [win[ctx_order[2 * s]][None], ada[n:n + 2], win[ctx_order[2 * s + 1]][None], ada[n + 2:n + 5]]
    stream0 = np.concatenate(parts)
    up, down = tiles(a["w_up"][0]), a["w_down"][0]
    parts = [wide_tiles(a["w_out"][0])]
    for e in range(EFF):
        parts += [halves(up[FT * e:FT * e + FT]), wide_tiles(down[FT * P * e:FT * P * (e + 1)])]
    stream2 = np.concatenate(parts)
    shift = a["rw_shift"][0].reshape(3, 21, P)
    par = np.stack([*shift[:, 6:12], *shift[:, 12:18], *shift[:, 0:6], *a["rw_w0"][0].reshape(2, 6, P),
                    *a["rw_a0"][0].reshape(2, 6, P), col(a["rw_kk"][0], 6), col(a["rw_ka"][0], 6),
                    a["rw_rk"][0].reshape(6, P), col(a["rw_gn_g"][0], 6), col(a["rw_gn_b"][0], 6)], -1)
    lp = shift[:, 18:21].transpose(2, 1, 0).reshape(P, 9)
    loraw = np.concatenate([a["rw_w2"][0].reshape(P, 6, P), a["rw_a2"][0].reshape(P, 6, P), a["rw_g2"][0].reshape(P, 6, P)],
                           2).transpose(1, 0, 2)
    cvec = np.stack([a["c"][0].reshape(KT, P), a["c_ctx"].reshape(KT, P)], -1).transpose(1, 0, 2).reshape(P, 2 * KT)
    head = np.kron(np.eye(2), np.ones((HD, HD))).astype(np.float32)
    small_both = np.concatenate([np.eye(P, dtype=np.float32), head], 1)
    small_first = np.concatenate([cvec, a["ada_b"][0].reshape(ADA_TILES, P).T,
                                  np.zeros((P, PAD_ADA - ADA_TILES), np.float32), lp, np.ones((P, P), np.float32)], 1)
    small_b = np.concatenate([triangles(), par.transpose(1, 0, 2).reshape(P, -1)], 1)
    agb = np.repeat(a["gm_bs"][0].reshape(APAIRS, 2, 1, P), HD, 2).reshape(APAIRS, P, P).transpose(1, 0, 2).reshape(P, -1)
    amix = np.concatenate([a["gm_ws"][0].transpose(2, 0, 1).reshape(P, 8 * P), agb], 1)
    r, c, kr, kc = np.ogrid[0:ROWS, 0:QC, 0:ROWS, 0:WC]
    per_block = []
    for b in range(4):
        dr = np.broadcast_to(kr - r + ROWS - 1, (ROWS, QC, ROWS, WC))
        dc = np.broadcast_to(np.clip(WIN0[b] + kc - QC * b - c + 15, 0, 30), (ROWS, QC, ROWS, WC))
        per_block.append(a["na_rpb"][0][:, dr, dc].reshape(6, 2, P, 256))
    bias = np.stack(per_block, 0).transpose(1, 3, 0, 2, 4).reshape(6, P, 8 * 256)
    lnrows = np.stack([a[n][0] for n in ("ln1_g", "ln1_b", "ln2_g", "ln2_b")])
    x = a["x"][0]
    arrays = dict(
        stream0=stream0, stream1=stream1, stream2=stream2, xT=x.T.reshape(KT, P, SEQ).transpose(1, 0, 2),
        ctxT=a["ctx"][0].T.reshape(KT, P, CTX).transpose(1, 0, 2), xtok=x.reshape(4, P, D).transpose(1, 0, 2),
        small_both=small_both, small_first=small_first, small_b=small_b, small_cmask=window_masks(), small_amix=amix,
        bias=bias, lnrows=lnrows, loraw=loraw)
    arrays = {k: f(v) for k, v in arrays.items()}

    nc = bacc.Bacc("TRN2", target_bir_lowering=False, num_devices=1)
    ap = {k: nc.dram_tensor(k, v.shape, F32, kind="ExternalInput").ap() for k, v in arrays.items()}
    out = nc.dram_tensor("out", (4, P, D), F32, kind="ExternalOutput").ap()
    small = {k[6:]: ap.pop(k) for k in list(ap) if k.startswith("small_")}
    build_block(nc, small=small, out=out, **ap)
    res = run_bass_kernel_spmd(nc, [arrays], core_ids=[0])
    return np.asarray(res.results[0]["out"]).reshape(1, SEQ, D)
```
